# Optimizing a Trainium2 kernel written in Bass

```python
import math
import jax, jax.numpy as jnp
from jax import lax
import numpy as np

D_MODEL = 1024
BATCH = 1
SEQ = 1024
DEPTH = 1

MIX_WIDTH = D_MODEL
RWKV_WIDTH = MIX_WIDTH // 2
RWKV_HEAD = 64
RWKV_HEADS = RWKV_WIDTH // RWKV_HEAD
DECAY_LORA = 64
ICL_LORA = 64
GATE_LORA = 128
GN_EPS = 64e-5
DIFF_WIDTH = MIX_WIDTH - RWKV_WIDTH
DIFF_HEAD = 64
DIFF_HEADS = DIFF_WIDTH // (2 * DIFF_HEAD)
DIFF_VDIM = 2 * DIFF_HEAD
Q_BLOCK = 128
RWKV_COLS = 3 * RWKV_WIDTH + DECAY_LORA + ICL_LORA + GATE_LORA
DIFF_COLS = 3 * DIFF_WIDTH
IN_COLS = RWKV_COLS + DIFF_COLS
N_EXPERTS = 32
TOP_K = 4
D_FF = D_MODEL
SWIGLU_ALPHA = 1.702
SWIGLU_LIMIT = 7.0
MOE_BLOCK = 128
NORM_EPS = 1e-5

kernel_name = 'hymba_rwkv7_diffattn_moe_layer'

def _rmsnorm(x, g, eps=NORM_EPS):
    xf = x.astype(jnp.float32)
    y = xf * lax.rsqrt(jnp.mean(xf * xf, axis=-1, keepdims=True) + eps)
    return (y * g.astype(jnp.float32)).astype(x.dtype)

def _alibi_slopes(n_heads):
    return 2.0 ** (-8.0 * (jnp.arange(n_heads, dtype=jnp.float32) + 1.0) / n_heads)

def _rwkv7_group(p, mu, w0, w_b, a0, a_b, g_b, k_k, k_a, r_k, ln_g, ln_b):
    bsz, seq, _ = p.shape
    f32 = jnp.float32
    prev = jnp.pad(p[:, :-1], ((0, 0), (1, 0), (0, 0)))
    p = p + (prev - p) * mu
    o1, o2, o3 = RWKV_WIDTH, 2 * RWKV_WIDTH, 3 * RWKV_WIDTH
    o4 = o3 + DECAY_LORA
    o5 = o4 + ICL_LORA
    r, k, v = p[..., :o1], p[..., o1:o2], p[..., o2:o3]
    w_lo, a_lo, g_lo = p[..., o3:o4], p[..., o4:o5], p[..., o5:]
    w = -jax.nn.softplus(-(w0 + jnp.tanh(w_lo) @ w_b).astype(f32)) - 0.5
    decay = jnp.exp(-jnp.exp(w))
    a = jax.nn.sigmoid(a0 + a_lo @ a_b)
    g = jax.nn.sigmoid(g_lo) @ g_b
    heads = lambda t: t.reshape(bsz, seq, RWKV_HEADS, RWKV_HEAD).astype(f32)
    kk = heads(k * k_k)
    kk = kk / jnp.maximum(jnp.sqrt(jnp.sum(kk * kk, axis=-1, keepdims=True)), 1e-12)
    k = k * (1.0 + (a - 1.0) * k_a)
    r_h, k_h, v_h, a_h, w_h = heads(r), heads(k), heads(v), heads(a), heads(decay)
    b_h = kk * a_h

    def step(state, inp):
        r_t, w_t, k_t, v_t, kk_t, b_t = inp
        sa = jnp.einsum('bhvk,bhk->bhv', state, kk_t)
        state = (state * w_t[:, :, None, :]
                 - sa[..., None] * b_t[:, :, None, :]
                 + v_t[..., None] * k_t[:, :, None, :])
        y_t = jnp.einsum('bhvk,bhk->bhv', state, r_t)
        return state, y_t

    xs = tuple(jnp.swapaxes(t, 0, 1) for t in (r_h, w_h, k_h, v_h, kk, b_h))
    state0 = jnp.zeros((bsz, RWKV_HEADS, RWKV_HEAD, RWKV_HEAD), f32)
    _, y = lax.scan(step, state0, xs)
    y = jnp.swapaxes(y, 0, 1)
    mean = jnp.mean(y, axis=-1, keepdims=True)
    var = jnp.mean(jnp.square(y - mean), axis=-1, keepdims=True)
    y = ((y - mean) * lax.rsqrt(var + GN_EPS)).reshape(bsz, seq, RWKV_WIDTH)
    y = y * ln_g.astype(f32) + ln_b.astype(f32)
    bonus = jnp.sum(r_h * k_h * r_k.astype(f32), axis=-1, keepdims=True) * v_h
    y = (y + bonus.reshape(bsz, seq, RWKV_WIDTH)) * g.astype(f32)
    return y.astype(p.dtype)

def _diff_attn_group(p, lq1, lk1, lq2, lk2, subln_g, lambda_init):
    bsz, seq, _ = p.shape
    f32 = jnp.float32
    q = p[..., :DIFF_WIDTH].reshape(bsz, seq, DIFF_HEADS, 2, DIFF_HEAD)
    k = p[..., DIFF_WIDTH:2 * DIFF_WIDTH].reshape(bsz, seq, DIFF_HEADS, 2, DIFF_HEAD)
    v = p[..., 2 * DIFF_WIDTH:].reshape(bsz, seq, DIFF_HEADS, DIFF_VDIM)
    lam = (jnp.exp(jnp.sum(lq1.astype(f32) * lk1.astype(f32)))
           - jnp.exp(jnp.sum(lq2.astype(f32) * lk2.astype(f32))) + lambda_init)
    slopes = _alibi_slopes(DIFF_HEADS)
    scale = DIFF_HEAD ** -0.5
    n_blocks = seq // Q_BLOCK
    q_blocks = jnp.swapaxes(q.reshape(bsz, n_blocks, Q_BLOCK, DIFF_HEADS, 2, DIFF_HEAD), 0, 1)
    k_pos = jnp.arange(seq)

    def block(args):
        q_blk, i = args
        s = jnp.einsum('bqhcd,bkhcd->bhcqk', q_blk, k).astype(f32) * scale
        q_pos = i * Q_BLOCK + jnp.arange(Q_BLOCK)
        dist = (q_pos[:, None] - k_pos[None, :]).astype(f32)
        s = s - slopes[None, :, None, None, None] * dist
        s = jnp.where(dist >= 0, s, -jnp.inf)
        pr = jax.nn.softmax(s, axis=-1)
        attn = pr[:, :, 0] - lam * pr[:, :, 1]
        return jnp.einsum('bhqk,bkhd->bqhd', attn.astype(v.dtype), v)

    o = lax.map(block, (q_blocks, jnp.arange(n_blocks)))
    o = jnp.swapaxes(o, 0, 1).reshape(bsz, seq, DIFF_HEADS, DIFF_VDIM)
    o = _rmsnorm(o, subln_g) * (1.0 - lambda_init)
    return o.reshape(bsz, seq, DIFF_WIDTH).astype(p.dtype)

def _moe(xn, router_w, router_b, w_up, b_up, w_down, b_down):
    bsz, seq, d = xn.shape
    xt = xn.reshape(-1, d)
    n_tok = xt.shape[0]
    logits = xt.astype(jnp.float32) @ router_w.astype(jnp.float32) + router_b.astype(jnp.float32)
    top_v, top_i = lax.top_k(logits, TOP_K)
    gate = jax.nn.softmax(top_v, axis=-1).astype(xt.dtype)
    n_assign = n_tok * TOP_K
    e_flat = top_i.reshape(n_assign)
    order = jnp.argsort(e_flat)
    e_sorted = e_flat[order]
    tok_sorted = (order // TOP_K).astype(jnp.int32)
    gate_sorted = gate.reshape(n_assign)[order]
    counts = jnp.bincount(e_flat, length=N_EXPERTS)
    start = jnp.cumsum(counts) - counts
    padded = (counts + MOE_BLOCK - 1) // MOE_BLOCK * MOE_BLOCK
    pad_end = jnp.cumsum(padded)
    pad_start = pad_end - padded
    dest = pad_start[e_sorted] + (jnp.arange(n_assign) - start[e_sorted])
    n_blocks = -(-n_assign // MOE_BLOCK) + N_EXPERTS
    n_slots = n_blocks * MOE_BLOCK
    slot_tok = jnp.zeros((n_slots,), jnp.int32).at[dest].set(tok_sorted)
    slot_gate = jnp.zeros((n_slots,), gate.dtype).at[dest].set(gate_sorted)
    blk_expert = jnp.minimum(
        jnp.searchsorted(pad_end, jnp.arange(n_blocks) * MOE_BLOCK, side='right'), N_EXPERTS - 1)

    def block(args):
        toks, gts, e = args
        h = xt[toks] @ w_up[e] + b_up[e]
        glu = jnp.minimum(h[:, ::2], SWIGLU_LIMIT)
        lin = jnp.clip(h[:, 1::2], -SWIGLU_LIMIT, SWIGLU_LIMIT)
        act = glu * jax.nn.sigmoid(SWIGLU_ALPHA * glu) * (lin + 1.0)
        y = act @ w_down[e] + b_down[e]
        return y * gts[:, None]

    ys = lax.map(block, (slot_tok.reshape(n_blocks, MOE_BLOCK),
                         slot_gate.reshape(n_blocks, MOE_BLOCK), blk_expert))
    out = jax.ops.segment_sum(ys.reshape(n_slots, d), slot_tok, num_segments=n_tok)
    return out.reshape(bsz, seq, d).astype(xn.dtype)

def setup_inputs(seed: int = 0) -> dict:
    key = jax.random.key(seed)
    ks = jax.random.split(key, 32)
    L, D, W = DEPTH, D_MODEL, RWKV_WIDTH
    nrm = lambda k, shape, s: jax.random.normal(k, shape, jnp.float32) * s
    return {
        'x': nrm(ks[0], (BATCH, SEQ, D), 1.0),
        'norm1_g': 1.0 + nrm(ks[1], (L, D), 0.05),
        'w_in': nrm(ks[2], (L, D, IN_COLS), D ** -0.5),
        'rwkv_mu': jax.random.uniform(ks[3], (L, RWKV_COLS), jnp.float32),
        'rwkv_w0': jax.random.uniform(ks[4], (L, W), jnp.float32, -6.0, 1.0),
        'rwkv_wb': nrm(ks[5], (L, DECAY_LORA, W), 0.5 * DECAY_LORA ** -0.5),
        'rwkv_a0': nrm(ks[6], (L, W), 0.1),
        'rwkv_ab': nrm(ks[7], (L, ICL_LORA, W), 0.5 * ICL_LORA ** -0.5),
        'rwkv_gb': nrm(ks[8], (L, GATE_LORA, W), GATE_LORA ** -0.5),
        'rwkv_kk': 0.85 + nrm(ks[9], (L, W), 0.05),
        'rwkv_ka': 1.0 + nrm(ks[10], (L, W), 0.05),
        'rwkv_rk': nrm(ks[11], (L, RWKV_HEADS, RWKV_HEAD), 0.1),
        'rwkv_ln_g': 1.0 + nrm(ks[12], (L, W), 0.05),
        'rwkv_ln_b': nrm(ks[13], (L, W), 0.01),
        'diff_lq1': nrm(ks[14], (L, DIFF_HEAD), 0.1),
        'diff_lk1': nrm(ks[15], (L, DIFF_HEAD), 0.1),
        'diff_lq2': nrm(ks[16], (L, DIFF_HEAD), 0.1),
        'diff_lk2': nrm(ks[17], (L, DIFF_HEAD), 0.1),
        'diff_subln_g': 1.0 + nrm(ks[18], (L, DIFF_VDIM), 0.05),
        'w_out': nrm(ks[19], (L, MIX_WIDTH, D), MIX_WIDTH ** -0.5),
        'norm2_g': 1.0 + nrm(ks[20], (L, D), 0.05),
        'router_w': nrm(ks[21], (L, D, N_EXPERTS), D ** -0.5),
        'router_b': nrm(ks[22], (L, N_EXPERTS), 0.01),
        'exp_w_up': nrm(ks[23], (L, N_EXPERTS, D, 2 * D_FF), D ** -0.5),
        'exp_b_up': nrm(ks[24], (L, N_EXPERTS, 2 * D_FF), 0.01),
        'exp_w_down': nrm(ks[25], (L, N_EXPERTS, D_FF, D), D_FF ** -0.5),
        'exp_b_down': nrm(ks[26], (L, N_EXPERTS, D), 0.01),
        'final_g': 1.0 + nrm(ks[27], (D,), 0.05),
    }

def reference(x, norm1_g, w_in, rwkv_mu, rwkv_w0, rwkv_wb, rwkv_a0, rwkv_ab, rwkv_gb,
              rwkv_kk, rwkv_ka, rwkv_rk, rwkv_ln_g, rwkv_ln_b, diff_lq1, diff_lk1,
              diff_lq2, diff_lk2, diff_subln_g, w_out, norm2_g, router_w, router_b,
              exp_w_up, exp_b_up, exp_w_down, exp_b_down, final_g):
    h = x
    for l in range(DEPTH):
        lambda_init = 0.8 - 0.6 * math.exp(-0.3 * l)
        xn = _rmsnorm(h, norm1_g[l])
        proj = xn @ w_in[l]
        y_rwkv = _rwkv7_group(proj[..., :RWKV_COLS], rwkv_mu[l], rwkv_w0[l], rwkv_wb[l],
                              rwkv_a0[l], rwkv_ab[l], rwkv_gb[l], rwkv_kk[l], rwkv_ka[l],
                              rwkv_rk[l], rwkv_ln_g[l], rwkv_ln_b[l])
        y_diff = _diff_attn_group(proj[..., RWKV_COLS:], diff_lq1[l], diff_lk1[l],
                                  diff_lq2[l], diff_lk2[l], diff_subln_g[l], lambda_init)
        h = h + jnp.concatenate([y_rwkv, y_diff], axis=-1) @ w_out[l]
        h = h + _moe(_rmsnorm(h, norm2_g[l]), router_w[l], router_b[l],
                     exp_w_up[l], exp_b_up[l], exp_w_down[l], exp_b_down[l])
    return _rmsnorm(h, final_g)


_drawn_inputs = setup_inputs


def setup_inputs(seed=0):
    import zlib

    import numpy as np

    out = dict(_drawn_inputs(seed))
    spreads = {}
    factors = {'rwkv_ln_b': 3.154, 'diff_lq1': 2.934, 'exp_b_up': 8.0, 'exp_b_down': 8.0}
    for name, (base, spread) in spreads.items():
        noise = np.random.default_rng([zlib.crc32(name.encode()), seed]).standard_normal(out[name].shape)
        drawn = base * np.exp(spread * noise) if base else spread * noise
        out[name] = __import__('jax').numpy.asarray(drawn.astype(out[name].dtype))
    for name, factor in factors.items():
        out[name] = (out[name] * factor).astype(out[name].dtype)
    return out
```

```python
import concourse.bass as bass
from concourse import mybir
from contextlib import ExitStack

P = 128
D = 1024
T = 1024
NT = T // P
KT = D // P
W = 512
CT = W // P
HD = 64
NG = W // HD
NE = 32
TOPK = 4
SLOTS = 2 * P
NSLOT = T * TOPK + SLOTS
MAXI = T * TOPK // SLOTS + NE
LEVELS = [1, 2, 4, 8, 16, 32]
NEG = -1.0e30
LAMBDA_INIT = 0.2
NORM_EPS = 1e-5
GN_EPS = 64e-5


def linker(eng, sem):
    count = [0]

    def link(ins):
        count[0] += 1
        ins.then_inc(sem, 1)
        eng.wait_ge(sem, count[0])
    return link


def inverse_root(dve, link, y, x, t, half):
    i32, ALU = mybir.dt.int32, mybir.AluOpType
    link(dve.tensor_scalar(half, x, -0.5, None, ALU.mult))
    link(dve.tensor_scalar(y.bitcast(i32), x.bitcast(i32), -0.5, float(0x5F3759DF), ALU.mult, ALU.add))
    for _ in range(3):
        link(dve.tensor_tensor(t, y, y, ALU.mult))
        link(dve.tensor_tensor(t, t, half, ALU.mult))
        link(dve.scalar_tensor_tensor(y, t, 1.5, y, ALU.add, ALU.mult))


def layer_program(nc, A, out):
    f32, f32r = mybir.dt.float32, mybir.dt.float32r
    i32, u32 = mybir.dt.int32, mybir.dt.uint32
    ALU, ACT, AX = mybir.AluOpType, mybir.ActivationFunctionType, mybir.AxisListType

    root = ExitStack()
    with root:
        def sem(name):
            return root.enter_context(nc.semaphore(name))

        def tile_in(stack):
            def sb(name, shape, dt=f32):
                return stack.enter_context(nc.sbuf_tensor(name, shape, dt))
            return sb

        sb = tile_in(root)
        PS = root.enter_context(nc.psum_tensor("PS", [P, 8, 512], f32))

        def pair(n):
            return PS[:, 2 * n:2 * n + 2, :].rearrange("p a n -> p (a n)")

        ident = sb("ident", [P, P])

        xn2_d = nc.dram_tensor("xn2_d", (T, D), f32).ap()
        h_d = nc.dram_tensor("h_d", (T, D), f32).ap()
        slot_d = nc.dram_tensor("slot_d", (NSLOT, 1), u32).ap()
        att_d = nc.dram_tensor("att_d", (P, CT, T), f32).ap()
        ys_d = nc.dram_tensor("ys_d", (NSLOT, D), f32).ap()
        pad_d = nc.dram_tensor("pad_d", (P, 2), u32).ap()
        item_d = nc.dram_tensor("item_d", (P, 4), i32).ap()

        small = ExitStack()
        mix = ExitStack()
        sb_small, sb_mix = tile_in(small), tile_in(mix)
        gates = sb("gates", [P, NT, TOPK])
        slots_u = sb("slots_u", [P, NT * TOPK], u32)

        ones = sb_small("ones", [P, P])
        later = sb_small("later", [P, P])
        rb_b = sb_small("rb_b", [P, NE])

        chunk1 = sb_mix("chunk1", [P, P])
        merge = sb_mix("merge", [P, len(LEVELS), P])
        causal2 = sb_mix("causal2", [P, 2, P])
        starts = sb_mix("starts", [P, 512])
        heads2 = sb_mix("heads2", [P, 2])
        mu_c = sb_mix("mu_c", [P, 14])
        omu_c = sb_mix("omu_c", [P, 14])
        par_c = sb_mix("par_c", [P, 5, CT])
        wab = sb_mix("wab", [P, W])
        gb = sb_mix("gb", [P, W])
        lng_b = sb_mix("lng_b", [P, W])
        lnb_b = sb_mix("lnb_b", [P, W])
        subg_b = sb_mix("subg_b", [P, P])
        hsel = sb_mix("hsel", [P, CT, NG])
        hspread = sb_mix("hspread", [NG, CT, P])
        lamt = sb_mix("lamt", [P, 8])

        rT = sb_mix("rT", [P, CT, T])
        kT = sb_mix("kT", [P, CT, T])
        vT = sb_mix("vT", [P, CT, T])
        loT = sb_mix("loT", [P, 2, T])
        big = sb_mix("big", [P, KT, T])
        xnT = big
        sgz, sga = big[:, 0:CT, :], big[:, CT:KT, :]

        att = ExitStack()
        sb_att = tile_in(att)
        qcT = sb_att("qcT", [P, CT, T])
        kcT = sb_att("kcT", [P, CT, T])
        vd = sb_att("vd", [P, NT, W])
        dist = sb_att("dist", [P, T])

        with ExitStack() as st:
            sbp = tile_in(st)
            wring = sbp("wring", [P, 2, KT, 512])
            xin = sbp("xin", [P, 2, D])
            g1b = sbp("g1b", [P, D])
            ssq = sbp("ssq", [P, NT])
            rstd = sbp("rstd", [P, 4, NT])
            scratch = vd.rearrange("p t n -> p (t n)")
            same = scratch[:, 0:(len(LEVELS) + 1) * P].rearrange("p (l n) -> p l n", n=P)
            lqk = scratch[:, 1024:1024 + 4 * HD].rearrange("p (l n) -> p l n", n=HD)
            s_msk, s_par, s_lam, s_mul, s_omu, s_id = (sem(n) for n in ("s_msk", "s_par", "s_lam", "s_mul", "s_omu", "s_id"))
            s_pc, s_dc, s_slot0, s_zero = (sem(n) for n in ("s_pc", "s_dc", "s_slot0", "s_zero"))
            s_g1, s_w0, s_w1 = sem("s_g1"), sem("s_w0"), sem("s_w1")
            s_xi = (sem("s_xi0"), sem("s_xi1"))
            s_sq, s_xs, s_tr, s_trA, s_trD = sem("s_sq"), sem("s_xs"), sem("s_tr"), sem("s_trA"), sem("s_trD")
            s_pj, s_evA, s_evD = sem("s_pj"), sem("s_evA"), sem("s_evD")
            s_c1 = sem("s_c1")
            s_wr = (s_w0, s_w1)
            SLABS = [(0, 512), (512, 512), (1024, 512), (1536, 512), (2048, 512), (2560, 256), (2816, 512)]
            CTILES = [(s, n) for s, (_, w) in enumerate(SLABS[:-1]) for n in range(w // P)]
            NC_ = len(CTILES)
            NR = 14
            x_rows = A["x"][0].rearrange("(j p) d -> j p d", p=P)
            w_in = A["w_in"][0].rearrange("(k p) n -> p k n", p=P)

            with nc.Block() as block:
                def evac_x(act, j):
                    act.wait_ge(s_tr, 2 * j + 1)
                    act.activation(xnT[:, 0:4, j * P:(j + 1) * P],
                                   PS[:, 2 * (j % 2), :].rearrange("p (a n) -> p a n", a=4), ACT.Copy).then_inc(s_trA, 1)

                def target(n):
                    return (rT[:, n % 4, :], kT[:, n % 4, :], vT[:, n % 4, :], loT[:, n % 2, :])[n // 4]

                @block.gpsimd
                def _(pool):
                    link = linker(pool, s_pc)
                    link(pool.memset(starts[:, :], 0.0))
                    link(pool.memset(ident[:, :], 0.0))
                    link(pool.affine_select(out=ident[:, :], in_=ident[:, :], compare_op=ALU.not_equal, fill=1.0,
                                            base=0, pattern=[[-1, P]], channel_multiplier=1))
                    pool.sem_inc(s_id, 1)
                    pool.sem_inc(s_zero, 1)
                    link(pool.memset(ones[:, :], 1.0))
                    link(pool.memset(same[:, :, :], 1.0))
                    for n in range(len(LEVELS) + 1):
                        b = 1 << n
                        v = same[:, n, :].rearrange("p (j b) -> p j b", b=b)
                        link(pool.affine_select(out=v, in_=v, compare_op=ALU.is_ge, fill=0.0, base=0,
                                                pattern=[[-b, P // b], [0, b]], channel_multiplier=1))
                        link(pool.affine_select(out=v, in_=v, compare_op=ALU.is_ge, fill=0.0, base=b - 1,
                                                pattern=[[b, P // b], [0, b]], channel_multiplier=-1))
                    link(pool.affine_select(out=later[:, :], in_=ones[:, :], compare_op=ALU.is_gt, fill=0.0,
                                            base=0, pattern=[[1, P]], channel_multiplier=-1))
                    chunk = same[:, len(LEVELS), :]
                    for n, op in enumerate((ALU.is_gt, ALU.is_ge)):
                        link(pool.affine_select(out=causal2[:, n, :], in_=chunk, compare_op=op, fill=0.0,
                                                base=0, pattern=[[1, P]], channel_multiplier=-1))
                    link(pool.tensor_copy(chunk1[:, :], chunk))
                    for n in range(len(LEVELS)):
                        link(pool.tensor_tensor(merge[:, n, :], same[:, n + 1, :], same[:, n, :], ALU.subtract))
                    link(pool.memset(hsel[:, :, :], 0.0))
                    for c in range(CT):
                        link(pool.tensor_copy(hsel[:, c, 2 * c:2 * c + 2], chunk.rearrange("p (a n) -> p a n", n=HD)[:, :, 0]))
                    link(pool.memset(hspread[:, :, :], 1.0))
                    link(pool.affine_select(out=hspread[:, :, :], in_=hspread[:, :, :], compare_op=ALU.is_ge, fill=0.0,
                                            base=0, pattern=[[P, CT], [1, P]], channel_multiplier=-HD))
                    link(pool.affine_select(out=hspread[:, :, :], in_=hspread[:, :, :], compare_op=ALU.is_ge, fill=0.0,
                                            base=HD - 1, pattern=[[-P, CT], [-1, P]], channel_multiplier=HD))
                    link(pool.tensor_copy(heads2[:, :], chunk.rearrange("p (a n) -> p a n", n=HD)[:, :, 0]))
                    pool.sem_inc(s_msk, 1)
                    link(pool.iota(dist[:, :].bitcast(i32), [[1, T]], base=-(T - P), channel_multiplier=-1))
                    link(pool.tensor_copy(dist[:, :], dist[:, :].bitcast(i32)))
                    link(pool.affine_select(out=dist[:, :], in_=dist[:, :], compare_op=ALU.is_ge, fill=NEG,
                                            base=T - P, pattern=[[-1, T]], channel_multiplier=1))

                @block.sync
                def _(sp):
                    sp.dma_start(g1b[:, :], A["norm1_g"][0].partition_broadcast(P)).then_inc(s_g1, 16)
                    for j in range(NT):
                        if j >= 2:
                            sp.wait_ge(s_tr, 2 * (j - 1))
                        sp.dma_start(xin[:, j % 2, :], x_rows[j]).then_inc(s_xi[j % 2], 16)
                        if j == 1:
                            for s in range(2):
                                c0, w = SLABS[s]
                                sp.dma_start(wring[:, s, :, 0:w], w_in[:, :, c0:c0 + w]).then_inc(s_wr[s], 16)
                    def col(v, n):
                        return v.rearrange("(c p) -> p c", p=P, c=n)
                    with nc.allow_non_contiguous_dma(reason="small parameters by channel"):
                        sp.dma_start(mu_c[:, :], col(A["rwkv_mu"][0], 14)).then_inc(s_par, 16)
                        rk = A["rwkv_rk"][0].rearrange("h d -> (h d)")
                        for n, v in enumerate((A["rwkv_w0"][0], A["rwkv_a0"][0], A["rwkv_kk"][0], A["rwkv_ka"][0], rk)):
                            sp.dma_start(par_c[:, n, :], col(v, CT)).then_inc(s_par, 16)
                    sp.dma_start(wab[0:64, :], A["rwkv_wb"][0]).then_inc(s_par, 16)
                    sp.dma_start(wab[64:128, :], A["rwkv_ab"][0]).then_inc(s_par, 16)
                    sp.dma_start(gb[:, :], A["rwkv_gb"][0]).then_inc(s_par, 16)
                    sp.dma_start(lng_b[:, :], A["rwkv_ln_g"][0].partition_broadcast(P)).then_inc(s_par, 16)
                    sp.dma_start(lnb_b[:, :], A["rwkv_ln_b"][0].partition_broadcast(P)).then_inc(s_par, 16)
                    sp.dma_start(subg_b[:, :], A["diff_subln_g"][0].partition_broadcast(P)).then_inc(s_par, 16)
                    for n, k in enumerate(("diff_lq1", "diff_lk1", "diff_lq2", "diff_lk2")):
                        sp.dma_start(lqk[:, n, :], A[k][0].partition_broadcast(P)).then_inc(s_par, 16)
                    sp.dma_start(rb_b[:, :], A["router_b"][0].partition_broadcast(P)).then_inc(s_par, 16)
                    sp.wait_ge(s_zero, 1)
                    n0 = NSLOT // P
                    sp.dma_start(slot_d.rearrange("(p n) a -> p (n a)", p=P),
                                 starts[:, 0:n0].bitcast(u32)).then_inc(s_slot0, 16)
                    for s in range(2, len(SLABS)):
                        c0, w = SLABS[s]
                        sp.wait_ge(s_pj, 1 + max(n for n, (t, _) in enumerate(CTILES) if t == s - 2))
                        sp.dma_start(wring[:, s % 2, :, 0:w], w_in[:, :, c0:c0 + w]).then_inc(s_wr[s % 2], 16)

                @block.scalar
                def _(act):
                    for j in range(NT):
                        act.wait_ge(s_xi[j % 2], 16 * (j // 2 + 1))
                        act.activation(pair(3), xin[:, j % 2, :], ACT.Square,
                                       accum_out=ssq[:, j:j + 1]).then_inc(s_sq, 1)
                        act.wait_ge(s_sq, j + 1)
                        if j >= 1:
                            evac_x(act, j - 1)
                    evac_x(act, NT - 1)
                    act.wait_ge(s_mul, 2)
                    act.activation(lamt[:, 2:4], lamt[:, 0:2], ACT.Exp).then_inc(s_lam, 1)
                    act.wait_ge(s_omu, 1)
                    for n, (s, _) in enumerate(CTILES):
                        act.wait_ge(s_pj, n + 1)
                        if n < NR:
                            dst = target(n)
                            act.activation(dst, pair(n % 4), ACT.Copy, scale=omu_c[:, n:n + 1]).then_inc(s_evA, 1)
                        elif n < NR + CT:
                            act.activation(qcT[:, n - NR, :], pair(n % 4), ACT.Copy,
                                           scale=float(HD) ** -0.5).then_inc(s_evA, 1)
                        else:
                            act.activation(kcT[:, n - NR - CT, :], pair(n % 4), ACT.Copy).then_inc(s_evA, 1)
                    act.wait_ge(s_msk, 1)
                    for j in range(NT):
                        act.wait_ge(s_pj, NC_ + j + 1)
                        act.activation(vd[:, j, :], PS[:, j % 8, :], ACT.Copy).then_inc(s_evA, 1)

                @block.vector
                def _(dve):
                    link = linker(dve, s_c1)
                    dve.wait_ge(s_g1, 16)
                    for j in range(NT):
                        dve.wait_ge(s_sq, j + 1)
                        r = [rstd[:, n, j:j + 1] for n in range(4)]
                        link(dve.tensor_scalar(r[1], ssq[:, j:j + 1], 1.0 / D, NORM_EPS, ALU.mult, ALU.add))
                        inverse_root(dve, link, *r)
                        dve.scalar_tensor_tensor(xin[:, j % 2, :], xin[:, j % 2, :], r[0], g1b[:, :],
                                                 ALU.mult, ALU.mult).then_inc(s_xs, 1)
                        dve.wait_ge(s_tr, 2 * j + 2)
                        dve.tensor_copy(xnT[:, 4:8, j * P:(j + 1) * P],
                                        PS[:, 2 * (j % 2) + 1, :].rearrange("p (a n) -> p a n", a=4)).then_inc(s_trD, 1)
                    tie = linker(dve, s_dc)
                    dve.wait_ge(s_par, 16 * 17)
                    tie(dve.tensor_scalar(omu_c[:, :], mu_c[:, :], -1.0, 1.0, ALU.mult, ALU.add))
                    dve.sem_inc(s_omu, 1)
                    tie(dve.tensor_scalar(subg_b[:, :], subg_b[:, :], 1.0 - LAMBDA_INIT, None, ALU.mult))
                    for n in range(2):
                        dve.tensor_tensor_reduce(out=lqk[:, 2 * n, :], in0=lqk[:, 2 * n, :], in1=lqk[:, 2 * n + 1, :],
                                                 scale=1.0, scalar=0.0, op0=ALU.mult, op1=ALU.add,
                                                 accum_out=lamt[:, n:n + 1]).then_inc(s_mul, 1)
                    dve.wait_ge(s_lam, 1)
                    tie(dve.tensor_tensor(lamt[:, 4:5], lamt[:, 3:4], lamt[:, 2:3], ALU.subtract))
                    tie(dve.tensor_scalar(lamt[:, 5:6], lamt[:, 4:5], -LAMBDA_INIT, None, ALU.add))
                    dve.wait_ge(s_slot0, 16)
                    tie(dve.memset(starts[:, :], 1.0))
                    tie(dve.memset(starts[:, :].rearrange("p (a n) -> p a n", n=HD)[:, :, 0], 0.0))
                    for n in range(NR):
                        dve.wait_ge(s_evA, n + 1)
                        dst = target(n)
                        dve.scalar_tensor_tensor(dst[:, 1:T], pair(n % 4)[:, 0:T - 1], mu_c[:, n:n + 1], dst[:, 1:T],
                                                 ALU.mult, ALU.add).then_inc(s_evD, 1)

                @block.tensor
                def _(pe):
                    pe.wait_ge(s_id, 1)
                    for j in range(NT):
                        pe.wait_ge(s_xs, j + 1)
                        if j >= 2:
                            pe.wait_ge(s_trA, j - 1)
                            pe.wait_ge(s_trD, j - 1)
                        for k in range(KT):
                            ins = pe.transpose(PS[:, 2 * (j % 2) + k // 4, (k % 4) * P:(k % 4 + 1) * P],
                                               xin[:, j % 2, k * P:(k + 1) * P], ident[:, :])
                            if k % 4 == 3:
                                ins.then_inc(s_tr, 1)
                    pe.wait_ge(s_trA, NT)
                    pe.wait_ge(s_trD, NT)
                    for n, (s, cc) in enumerate(CTILES):
                        if cc == 0:
                            pe.wait_ge(s_wr[s % 2], 16 * (s // 2 + 1))
                        if n >= 4:
                            pe.wait_ge(s_evA, n - 3)
                            pe.wait_ge(s_evD, min(n - 3, NR))
                        for th in range(2):
                            for k in range(KT):
                                ins = pe.matmul(PS[:, 2 * (n % 4) + th, :], wring[:, s % 2, k, cc * P:(cc + 1) * P],
                                                xnT[:, k, th * 512:(th + 1) * 512], start=(k == 0), stop=(k == KT - 1))
                        ins.then_inc(s_pj, 1)
                    s = len(SLABS) - 1
                    pe.wait_ge(s_wr[s % 2], 16 * (s // 2 + 1))
                    pe.wait_ge(s_evA, NC_)
                    for j in range(NT):
                        for k in range(KT):
                            ins = pe.matmul(PS[:, j % 8, :], xnT[:, k, j * P:(j + 1) * P], wring[:, s % 2, k, :],
                                            start=(k == 0), stop=(k == KT - 1))
                        ins.then_inc(s_pj, 1)

        UN = NT * CT
        with ExitStack() as st:
            sba = tile_in(st)
            alibi = sba("alibi", [P, CT, T])
            sc2 = sba("sc2", [P, 2, T])
            scs = (big[:, CT:CT + 2, :], big[:, CT + 2:CT + 4, :], sc2)
            aT = sba("aT", [P, 2, NT, P])
            osb = sba("osb", [P, 2, CT, P])
            st8 = sba("st8", [P, 2, 6])
            fac = sba("fac", [P, 4, 2])
            no2 = sba("no2", [P, 5, CT])
            osq = sba("osq", [P, P])
            attT = big[:, 0:CT, :]
            a_dc, a_al = sem("a_dc"), sem("a_al")
            a_s, a_mx, a_ex, a_cb, a_t, a_te = (sem(n) for n in ("a_s", "a_mx", "a_ex", "a_cb", "a_t", "a_te"))
            a_o, a_oe, a_sq, a_n, a_f, a_fe = (sem(n) for n in ("a_o", "a_oe", "a_sq", "a_n", "a_f", "a_fe"))
            a_nm, a_out, a_nr = sem("a_nm"), sem("a_out"), sem("a_nr")
            with nc.Block() as block:
                @block.sync
                def _(sp):
                    for i in range(NT):
                        sp.wait_ge(a_fe, i + 1)
                        sp.dma_start(att_d[:, :, i * P:(i + 1) * P], attT[:, :, i * P:(i + 1) * P]).then_inc(a_out, 16)
                    sp.wait_ge(a_out, 16 * NT)

                def width(n):
                    return (n // CT + 1) * P

                @block.tensor
                def _(pe):
                    def scores(n):
                        i, h = n // CT, n % CT
                        if n >= 1:
                            pe.wait_ge(a_mx, 2 * n)
                        for m in range(2):
                            for c0 in range(0, width(n), 512):
                                w = min(512, width(n) - c0)
                                ins = pe.matmul(PS[:, 2 * m + c0 // 512, 0:w], qcT[64 * m:64 * m + 64, h, i * P:(i + 1) * P],
                                                kcT[64 * m:64 * m + 64, h, c0:c0 + w], start=True, stop=True)
                        ins.then_inc(a_s, 1)

                    def turn(n):
                        i = n // CT
                        pe.wait_ge(a_cb, n + 1)
                        if n >= 1:
                            pe.wait_ge(a_te, n)
                        for k in range(i + 1):
                            ins = pe.transpose(PS[:, 4 + k // 4, (k % 4) * P:(k % 4 + 1) * P],
                                               scs[n % 3][:, 0, k * P:(k + 1) * P], ident[:, :])
                        ins.then_inc(a_t, 1)

                    def values(n):
                        i, h = n // CT, n % CT
                        pe.wait_ge(a_te, n + 1)
                        if n >= 1:
                            pe.wait_ge(a_oe, n)
                        for k in range(i + 1):
                            ins = pe.matmul(PS[:, 6, 0:P], aT[:, n % 2, k, :], vd[:, k, h * P:(h + 1) * P],
                                            start=(k == 0), stop=(k == i))
                        ins.then_inc(a_o, 1)

                    def flip(i):
                        pe.wait_ge(a_n, CT * (i + 1))
                        if i >= 1:
                            pe.wait_ge(a_fe, i)
                        for h in range(CT):
                            ins = pe.transpose(PS[:, 7, h * P:(h + 1) * P], osb[:, i % 2, h, :], ident[:, :])
                        ins.then_inc(a_f, 1)

                    scores(0)
                    for n in range(UN):
                        if n + 1 < UN:
                            scores(n + 1)
                        if n >= 1:
                            turn(n - 1)
                        if n >= 2:
                            values(n - 2)
                        if n >= CT and n % CT == 3:
                            flip(n // CT - 1)
                    turn(UN - 1)
                    values(UN - 2)
                    values(UN - 1)
                    flip(NT - 1)

                @block.vector
                def _(dve):
                    link = linker(dve, a_dc)
                    def maxima(n):
                        i, h = n // CT, n % CT
                        dve.wait_ge(a_s, n + 1)
                        dve.wait_ge(a_al, h + 1)
                        if n >= 3:
                            dve.wait_ge(a_t, n - 2)
                        w = width(n)
                        for m in range(2):
                            dve.tensor_tensor_reduce(out=scs[n % 3][:, m, 0:w], in0=pair(m)[:, 0:w],
                                                     in1=alibi[:, h, T - w:T], scale=1.0, scalar=NEG, op0=ALU.add, op1=ALU.max,
                                                     accum_out=st8[:, n % 2, m:m + 1]).then_inc(a_mx, 1)
                        dve.wait_ge(a_mx, 2 * n + 2)
                        dve.tensor_scalar(st8[:, n % 2, 2:4], st8[:, n % 2, 0:2], -1.0, None, ALU.mult).then_inc(a_nm, 1)

                    def combine(n):
                        w = width(n)
                        dve.wait_ge(a_ex, 2 * n + 2)
                        sums, f = st8[:, n % 2, 4:6], fac[:, n % 4, :]
                        link(dve.reciprocal(f[:, 0:2], sums))
                        link(dve.scalar_tensor_tensor(f[:, 1:2], f[:, 1:2], lamt[:, 5:6], sums[:, 0:1], ALU.mult, ALU.mult))
                        dve.scalar_tensor_tensor(scs[n % 3][:, 0, 0:w], scs[n % 3][:, 1, 0:w], f[:, 1:2],
                                                 scs[n % 3][:, 0, 0:w], ALU.mult, ALU.add).then_inc(a_cb, 1)

                    def norm(i):
                        dve.wait_ge(a_sq, CT * (i + 1))
                        t = [no2[:, n, :] for n in range(5)]
                        dve.tensor_scalar(t[2], t[0], 1.0 / P, NORM_EPS, ALU.mult, ALU.add).then_inc(a_nr, 1)
                        dve.wait_ge(a_nr, i + 1)
                        inverse_root(dve, link, *t[1:])
                        for h in range(CT):
                            dve.scalar_tensor_tensor(osb[:, i % 2, h, :], osb[:, i % 2, h, :], t[1][:, h:h + 1], subg_b[:, :],
                                                     ALU.mult, ALU.mult).then_inc(a_n, 1)

                    maxima(0)
                    for n in range(UN):
                        if n + 1 < UN:
                            maxima(n + 1)
                        combine(n)
                        if n >= CT and n % CT == 2:
                            norm(n // CT - 1)
                    norm(NT - 1)

                @block.scalar
                def _(act):
                    def exps(n):
                        act.wait_ge(a_nm, n + 1)
                        for m in range(2):
                            v = scs[n % 3][:, m, 0:width(n)]
                            act.activation(v, v, ACT.Exp, bias=st8[:, n % 2, 2 + m:3 + m],
                                           accum_out=st8[:, n % 2, 4 + m:5 + m]).then_inc(a_ex, 1)

                    def keys(n):
                        i = n // CT
                        act.wait_ge(a_t, n + 1)
                        if n >= 2:
                            act.wait_ge(a_o, n - 1)
                        flat = aT[:, n % 2, 0:i + 1, :].rearrange("p a n -> p (a n)")
                        act.activation(flat, pair(2)[:, 0:width(n)], ACT.Copy).then_inc(a_te, 1)

                    def rows(n):
                        i, h = n // CT, n % CT
                        act.wait_ge(a_o, n + 1)
                        if i >= 2:
                            act.wait_ge(a_f, i - 1)
                        act.activation(osb[:, i % 2, h, :], PS[:, 6, 0:P], ACT.Copy, scale=fac[:, n % 4, 0:1]).then_inc(a_oe, 1)
                        act.wait_ge(a_oe, n + 1)
                        if i >= 1:
                            act.wait_ge(a_nr, i)
                        act.activation(osq[:, :], osb[:, i % 2, h, :], ACT.Square,
                                       accum_out=no2[:, 0, h:h + 1]).then_inc(a_sq, 1)
                        act.wait_ge(a_sq, n + 1)

                    def done(i):
                        act.wait_ge(a_f, i + 1)
                        act.activation(attT[:, :, i * P:(i + 1) * P], PS[:, 7, :].rearrange("p (c n) -> p c n", c=CT),
                                       ACT.Copy).then_inc(a_fe, 1)

                    for h in range(CT):
                        act.activation(alibi[:, h, :], dist[:, :], ACT.Copy, scale=2.0 ** (-8.0 * (h + 1) / CT)).then_inc(a_al, 1)
                    exps(0)
                    for n in range(UN):
                        if n + 1 < UN:
                            exps(n + 1)
                        if n >= 1:
                            keys(n - 1)
                        if n >= 2:
                            rows(n - 2)
                        if n >= 2 * CT and n % CT == 0:
                            done(n // CT - 2)
                    keys(UN - 1)
                    rows(UN - 2)
                    done(NT - 2)
                    rows(UN - 1)
                    done(NT - 1)
        att.close()

        def head_of(g):
            return 2 * (g % CT) + g // CT

        with ExitStack() as st:
            sbr = tile_in(st)
            cum, eL, eU, eN = (sbr(n, [P, CT, P]) for n in ("cum", "eL", "eU", "eN"))
            ld = eL
            kk, kn, be, ka = (sbr(n, [P, CT, P]) for n in ("kk", "kn", "be", "ka"))
            ar = sbr("ar", [P, 2, CT, 2, P])
            rkp = sbr("rkp", [P, 2, CT, P])
            pc = sbr("pc", [P, 2, CT, 2])
            tok = sbr("tok", [P, 2, 2, W])
            BG = sbr("BG", [P, 2, NG, 2, P])
            KG = sbr("KG", [P, 2, NG, 2, P])
            LM = sbr("LM", [P, 2, NG, P])
            XT = sbr("XT", [P, 2, NG, P])
            X = sbr("X", [P, NG, P])
            PM = sbr("PM", [P, NG, P])
            S = sbr("S", [P, CT, P])
            Rb, Un = loT[:, 0, 0:W], loT[:, 0, W:2 * W]
            ysb = sbr("ysb", [P, W])
            gn = sbr("gn", [P, 4, NG])
            Sq = wab[:, :].rearrange("p (h n) -> p h n", n=HD)
            rn = sbr("rn", [NG, T])
            gr = sbr("gr", [P, 3, NG])
            r_s8, r_n8, r_rt, r_ri = sem("r_s8"), sem("r_n8"), sem("r_rt"), sem("r_ri")
            NL = len(LEVELS)
            r_dc, r_pc, r_ac = sem("r_dc"), sem("r_pc"), sem("r_ac")
            r_act, r_z, r_ze = sem("r_act"), sem("r_z"), sem("r_ze")
            r_cum, r_exp, r_kr, r_sq, r_ss, r_rn = (sem(n) for n in ("r_cum", "r_exp", "r_kr", "r_sq", "r_ss", "r_rn"))
            r_kp, r_pD, r_pP, r_tr, r_te, r_g, r_ge = (sem(n) for n in ("r_kp", "r_pD", "r_pP", "r_tr", "r_te", "r_g", "r_ge"))
            r_lm, r_x0, r_P, r_Pe, r_X, r_Xe, r_T, r_Te = (sem(n) for n in ("r_lm", "r_x0", "r_P", "r_Pe", "r_X", "r_Xe", "r_T", "r_Te"))
            q_0, q_R, q_Re, q_U, q_Ue, q_S, q_Se, q_Y = (sem(n) for n in ("q_0", "q_R", "q_Re", "q_U", "q_Ue", "q_S", "q_Se", "q_Y"))
            q_y1, q_bg, q_y2, q_f, q_yT, q_pcw = (sem(n) for n in ("q_y1", "q_bg", "q_y2", "q_f", "q_yT", "q_pcw"))

            def cut(a, i):
                return a[:, :, i * P:(i + 1) * P]

            def by_c(n):
                return par_c[:, n, :].unsqueeze(2).to_broadcast([P, CT, P])

            def over_heads(m, n):
                return m.unsqueeze(1).to_broadcast([P, n, P])

            with nc.Block() as block:
                @block.tensor
                def _(pe):
                    pe.wait_ge(r_act, 1)
                    for n in range(2 * CT):
                        c, th = n // 2, n % 2
                        if n >= 4:
                            pe.wait_ge(r_ze, 2 * (n - 3))
                        for a in range(2):
                            pe.matmul(PS[:, 4 * a + n % 4, :], wab[64 * a:64 * a + 64, c * P:(c + 1) * P],
                                      loT[64 * a:64 * a + 64, 0, th * 512:(th + 1) * 512],
                                      start=True, stop=True).then_inc(r_z, 1)
                    pe.wait_ge(r_ze, 4 * CT)

                    for n in range(2 * CT):
                        th, c = n // CT, n % CT
                        pe.wait_ge(r_s8, n + 1)
                        pe.matmul(PS[0:NG, th, :], hsel[:, c, :], (kn, be)[n % 2][:, :, :].rearrange("p c n -> p (c n)"),
                                  start=(c == 0), stop=(c == CT - 1)).then_inc(r_n8, 1)
                    pe.wait_ge(r_ri, 1)

                    def norms(i):
                        if i >= 3:
                            pe.wait_ge(q_y2, i - 2)
                        for c in range(CT):
                            ins = pe.matmul(PS[:, 6, c * P:(c + 1) * P], hspread[:, c, :], rn[:, i * P:(i + 1) * P],
                                            start=True, stop=True)
                        ins.then_inc(r_ss, 1)

                    def grams(i):
                        pe.wait_ge(r_pD, i + 1)
                        pe.wait_ge(r_pP, i + 1)
                        if i >= 1:
                            pe.wait_ge(r_Te, 2 * (NL) * i)
                            pe.wait_ge(r_Xe, 2 * (NL - 1) * i)
                        for n, src in enumerate((be, ka, None)):
                            for c in range(CT):
                                v = src[:, c, :] if src is not None else vT[:, c, i * P:(i + 1) * P]
                                ins = pe.transpose(PS[:, 1 + n, c * P:(c + 1) * P], v, ident[:, :])
                            ins.then_inc(r_tr, 1)
                        for n, src in enumerate((be, ka)):
                            for g in range(NG):
                                b, hp, c = g // 2, g // CT, g % CT
                                if g % 2 == 0:
                                    if n == 0 and b > 0:
                                        pe.wait_ge(r_te, 3 * i + b)
                                    if n == 1:
                                        pe.wait_ge(r_ge, 8 * i + b + 1)
                                ins = pe.matmul(PS[:, b, (g % 2) * 256:(g % 2) * 256 + 256],
                                                src[64 * hp:64 * hp + 64, c, :],
                                                ar[64 * hp:64 * hp + 64, i % 2, c, :, :].rearrange("p a n -> p (a n)"),
                                                start=True, stop=True)
                                if g % 2 == 1:
                                    ins.then_inc(r_g, 1)

                    def flip(i, l, src):
                        for hf in range(2):
                            if l == 0:
                                pe.wait_ge(r_x0, i + 1)
                                pe.wait_ge(r_ge, 8 * i + 8)
                            else:
                                pe.wait_ge(r_Xe, 2 * (NL - 1) * i + 2 * (l - 1) + hf + 1)
                                pe.wait_ge(r_Pe, 2 * (NL - 1) * i + 2 * (l - 1) + hf + 1)
                            for g in range(4 * hf, 4 * hf + 4):
                                ins = pe.transpose(PS[:, hf, (g % 4) * P:(g % 4 + 1) * P], src[:, g, :], ident[:, :])
                            ins.then_inc(r_T, 1)

                    def level_P(i, l):
                        pe.wait_ge(r_lm, NL * i + l + 1)
                        for hf in range(2):
                            pe.wait_ge(r_Te, 2 * NL * i + 2 * l - 1 + hf)
                            for g in range(4 * hf, 4 * hf + 4):
                                ins = pe.matmul(PS[:, hf, (g % 4) * P:(g % 4 + 1) * P], LM[:, l % 2, g, :], X[:, g, :],
                                                start=True, stop=True)
                            ins.then_inc(r_P, 1)

                    def level_X(i, l):
                        for hf in range(2):
                            pe.wait_ge(r_Pe, 2 * (NL - 1) * i + 2 * (l - 1) + hf + 1)
                            if l >= 2:
                                pe.wait_ge(r_Xe, 2 * (NL - 1) * i + 2 * (l - 2) + hf + 1)
                            for g in range(4 * hf, 4 * hf + 4):
                                ins = pe.matmul(PS[:, 2 + hf, (g % 4) * P:(g % 4 + 1) * P], XT[:, i % 2, g, :],
                                                PM[:, g, :], start=True, stop=True)
                            ins.then_inc(r_X, 1)

                    def state_term(i, cp, half, bank, **kw):
                        for c in range(CT):
                            ins = pe.matmul(PS[64 * cp:64 * cp + 64, bank, c * P:(c + 1) * P],
                                            ar[:, i % 2, c, half, 64 * cp:64 * cp + 64], S[:, c, :],
                                            start=False, stop=True, skip_group_check=True)
                        return ins

                    def head_term(i, bank, lhs, rhs, first):
                        for g in range(NG):
                            h = head_of(g)
                            ins = pe.matmul(PS[:, bank, h * HD:(h + 1) * HD], lhs(g),
                                            rhs[:, h // 2, (h % 2) * HD:(h % 2 + 1) * HD],
                                            start=(first and g == 0), stop=True, skip_group_check=True)
                        return ins

                    def seq(i, s):
                        q = i % 2
                        v = cut(vT, i)
                        if s == 0:
                            pe.wait_ge(q_0, 1)
                            pe.wait_ge(r_ge, 8 * i + 8)
                            pe.wait_ge(r_te, 3 * i + 3)
                            if i >= 1:
                                pe.wait_ge(q_yT, i)
                                pe.wait_ge(q_Se, 4 * i)
                            head_term(i, 4, lambda g: KG[:, q, g, 0, :], v, True)
                            state_term(i, 0, 0, 4).then_inc(q_R, 1)
                        if s in (1, 4):
                            cp = s // 4
                            pe.wait_ge(q_Re, 2 * i + cp + 1)
                            pe.wait_ge(r_Te, 2 * NL * (i + 1))
                            if i >= 1:
                                pe.wait_ge(q_y2, i)
                            for g in range(NG):
                                h = head_of(g)
                                ins = pe.matmul(PS[64 * cp:64 * cp + 64, 5, h * HD:(h + 1) * HD],
                                                XT[:, q, g, 64 * cp:64 * cp + 64], Rb[:, h * HD:(h + 1) * HD],
                                                start=True, stop=True)
                            ins.then_inc(q_U, 1)
                            if s == 1:
                                if i >= 1:
                                    pe.wait_ge(q_y1, i)
                                head_term(i, 7, lambda g: KG[:, q, g, 1, :], v, True)
                            state_term(i, cp, 1, 7)
                        if s in (2, 5):
                            cp = s // 5
                            rows = slice(64 * cp, 64 * cp + 64)
                            pe.wait_ge(q_Ue, 2 * i + cp + 1)
                            if i + 2 < NT:
                                pe.wait_ge(r_rn, i + 3)
                            if cp:
                                pe.wait_ge(q_Se, 4 * i + 2)
                            for c in range(CT):
                                cols = slice(c * P, (c + 1) * P)
                                pe.matmul(PS[:, 6, cols], tok[rows, q, 1, cols], v[rows, c, :],
                                          start=(c == 0), stop=False, skip_group_check=True)
                            for c in range(CT):
                                cols = slice(c * P, (c + 1) * P)
                                ins = pe.matmul(PS[:, 6, cols], tok[rows, q, 0, cols], Un[rows, cols],
                                                start=False, stop=True, skip_group_check=True)
                            ins.then_inc(q_S, 1)
                            if cp:
                                head_term(i, 7, lambda g: BG[:, q, g, 1, :],
                                          Un[:, :].rearrange("p (c n) -> p c n", c=CT), False).then_inc(q_Y, 1)
                        if s == 3:
                            pe.wait_ge(q_Se, 4 * i + 2)
                            pe.wait_ge(q_Re, 2 * i + 1)
                            state_term(i, 1, 0, 4).then_inc(q_R, 1)
                        if s == 6:
                            pe.wait_ge(q_Se, 4 * i + 4)
                            pe.wait_ge(q_Ue, 2 * i + 2)
                            for c in range(CT):
                                pe.matmul(PS[:, 6, 2 * c:2 * c + 2], rkp[:, q, c, :], heads2[:, :], start=True, stop=True)
                            pe.matmul(PS[:, 5, :], loT[:, 1, i * P:(i + 1) * P], gb[:, :],
                                      start=True, stop=True).then_inc(q_bg, 1)
                        if s == 7:
                            pe.wait_ge(q_y2, i + 1)
                            pe.wait_ge(q_Re, 2 * i + 2)
                            for c in range(CT):
                                ins = pe.transpose(PS[:, 4, c * P:(c + 1) * P], ysb[:, c * P:(c + 1) * P], ident[:, :])
                            ins.then_inc(q_f, 1)

                    norms(0)
                    for i in range(NT):
                        grams(i)
                        flip(i, 0, XT[:, i % 2])
                        for l in range(1, NL):
                            level_P(i, l)
                            if l == 1 and i + 1 < NT:
                                norms(i + 1)
                            if i >= 1 and l <= 3:
                                seq(i - 1, 2 * l - 2)
                            if i >= 1 and l == 4:
                                seq(i - 1, 6)
                            level_X(i, l)
                            if i >= 1 and l <= 3:
                                seq(i - 1, 2 * l - 1)
                            flip(i, l, X)
                        if i >= 1:
                            seq(i - 1, 7)
                    for s in range(8):
                        seq(NT - 1, s)

                @block.scalar
                def _(act):
                    link = linker(act, r_ac)
                    act.activation(loT[0:64, 0, :], loT[0:64, 0, :], ACT.Tanh).then_inc(r_act, 1)
                    link(act.activation(loT[:, 1, :], loT[:, 1, :], ACT.Sigmoid))
                    for n in range(2 * CT):
                        c, th = n // 2, n % 2
                        for a in range(2):
                            act.wait_ge(r_z, 2 * n + a + 1)
                            act.activation((sgz, sga)[a][:, c, th * 512:(th + 1) * 512], PS[:, 4 * a + n % 4, :],
                                           ACT.Sigmoid, bias=par_c[:, a, c:c + 1]).then_inc(r_ze, 1)

                    for n in range(2 * CT):
                        th, c = n // CT, n % CT
                        if n >= 2:
                            act.wait_ge(r_n8, n - 1)
                        act.activation((kn, be)[n % 2][:, :, :].rearrange("p c n -> p (c n)"),
                                       kT[:, c, th * 512:(th + 1) * 512], ACT.Square,
                                       scale=par_c[:, 2, c:c + 1]).then_inc(r_s8, 1)
                    act.wait_ge(r_n8, 2 * CT)
                    act.activation(rn[:, :], pair(0)[0:NG, :], ACT.Sqrt).then_inc(r_rt, 1)

                    def exps(i):
                        act.wait_ge(r_cum, i + 1)
                        if i >= 1:
                            act.wait_ge(r_pD, i)
                            act.wait_ge(r_pP, i)
                        act.activation(eU[:, :, :], cum[:, :, :], ACT.Exp).then_inc(r_exp, 1)
                        act.activation(eN[:, :, :], cum[:, :, :], ACT.Exp, scale=-1.0).then_inc(r_exp, 1)
                        act.activation(eL[:, :, :], eL[:, :, :], ACT.Exp).then_inc(r_exp, 1)

                    def seq(i, s):
                        q = i % 2
                        if s in (1, 4):
                            cp = s // 4
                            rows = slice(64 * cp, 64 * cp + 64)
                            act.wait_ge(q_U, 2 * i + cp + 1)
                            if i >= 1:
                                act.wait_ge(q_Y, i)
                            act.activation(Un[rows, :], PS[rows, 5, :], ACT.Copy, scale=-1.0).then_inc(q_Ue, 1)
                        if s == 5:
                            act.wait_ge(q_Y, i + 1)
                            if i >= 1:
                                act.wait_ge(q_f, i)
                            act.activation(ysb[:, :], PS[:, 7, :], ACT.Copy).then_inc(q_y1, 1)
                        if s == 7:
                            act.wait_ge(q_f, i + 1)
                            act.activation(cut(rT, i), PS[:, 4, :].rearrange("p (c n) -> p c n", c=CT),
                                           ACT.Copy).then_inc(q_yT, 1)

                    exps(0)
                    for i in range(NT):
                        q = i % 2
                        for n in range(3):
                            act.wait_ge(r_tr, 3 * i + n + 1)
                            if i >= 2:
                                act.wait_ge(q_y2, i - 1)
                            dst = tok[:, q, n, :].rearrange("p (c n) -> p c n", c=CT) if n < 2 else cut(vT, i)
                            act.activation(dst, PS[:, 1 + n, :].rearrange("p (c n) -> p c n", c=CT),
                                           ACT.Copy).then_inc(r_te, 1)
                        for hf in range(2):
                            act.wait_ge(r_T, 2 * NL * i + hf + 1)
                            act.activation(X[:, 4 * hf:4 * hf + 4, :], PS[:, hf, :].rearrange("p (c n) -> p c n", c=4),
                                           ACT.Copy).then_inc(r_Te, 1)
                        for l in range(1, NL):
                            for hf in range(2):
                                act.wait_ge(r_P, 2 * (NL - 1) * i + 2 * (l - 1) + hf + 1)
                                act.activation(PM[:, 4 * hf:4 * hf + 4, :],
                                               PS[:, hf, :].rearrange("p (c n) -> p c n", c=4), ACT.Copy).then_inc(r_Pe, 1)
                            if l == 1 and i + 1 < NT:
                                exps(i + 1)
                            if i >= 1 and l <= 3:
                                seq(i - 1, 2 * l - 2)
                                seq(i - 1, 2 * l - 1)
                            for hf in range(2):
                                act.wait_ge(r_T, 2 * NL * i + 2 * l + hf + 1)
                                act.activation(XT[:, q, 4 * hf:4 * hf + 4, :],
                                               PS[:, hf, :].rearrange("p (c n) -> p c n", c=4), ACT.Copy).then_inc(r_Te, 1)
                        if i >= 1:
                            seq(i - 1, 7)
                    for s in range(8):
                        seq(NT - 1, s)

                @block.gpsimd
                def _(pool):
                    link = linker(pool, r_pc)
                    link(pool.memset(S[:, :, :], 0.0))
                    pool.wait_ge(r_ze, 4 * CT)
                    link(pool.memset(Rb[:, :], 0.0))
                    pool.sem_inc(q_0, 1)

                    def raw(i):
                        if i >= 1:
                            pool.wait_ge(r_pD, i)
                        else:
                            pool.wait_ge(r_ri, 1)
                        pool.tensor_tensor(kk[:, :, :], cut(kT, i), by_c(2), ALU.mult).then_inc(r_kr, 1)

                    def rho(i):
                        pool.wait_ge(r_exp, 3 * i + 1)
                        if i >= 2:
                            pool.wait_ge(q_S, 2 * (i - 1))
                            pool.wait_ge(q_Se, 4 * (i - 1))
                            pool.wait_ge(q_bg, i - 1)
                        pool.tensor_tensor(ar[:, i % 2, :, 1, :], cut(rT, i), eU[:, :, :], ALU.mult).then_inc(q_pcw, 1)
                        link(pool.tensor_copy(pc[:, i % 2, :, :], eU[:, :, :].rearrange("p c (a n) -> p c a n", n=HD)[:, :, :, HD - 1]))
                        pool.wait_ge(r_kp, i + 1)
                        link(pool.tensor_tensor(rkp[:, i % 2, :, :], cut(rT, i), by_c(4), ALU.mult))
                        pool.wait_ge(q_pcw, i + 1)
                        pool.tensor_tensor(rkp[:, i % 2, :, :], rkp[:, i % 2, :, :], kn[:, :, :], ALU.mult).then_inc(r_pP, 1)

                    def part(i, l):
                        if l == 0:
                            pool.wait_ge(r_ge, 8 * i + 4)
                        if l == 2:
                            pool.wait_ge(r_x0, i + 1)
                        if l != 2 and (i or l > 2):
                            pool.wait_ge(r_P, 2 * (NL - 1) * i + 2 * (l - 2) if l > 2 else 2 * (NL - 1) * i - 2 * (1 - l))
                        pool.tensor_tensor(LM[:, l % 2, :, :], BG[:, i % 2, :, 0, :], over_heads(merge[:, l, :], NG),
                                           ALU.mult).then_inc(r_lm, 1)

                    raw(0)
                    rho(0)
                    for i in range(NT):
                        if i + 1 < NT:
                            raw(i + 1)
                        for l in range(NL):
                            part(i, l)
                            if l == NL - 1 and i + 1 < NT:
                                rho(i + 1)

                @block.vector
                def _(dve):
                    link = linker(dve, r_dc)
                    dve.wait_ge(r_ze, 4 * CT)
                    dve.wait_ge(r_rt, 1)
                    link(dve.tensor_scalar(rn[:, :], rn[:, :], 1e-12, None, ALU.max))
                    dve.reciprocal(rn[:, :], rn[:, :]).then_inc(r_ri, 1)

                    def decay(i):
                        if i >= 1:
                            dve.wait_ge(r_exp, 3 * i)
                            dve.wait_ge(r_pD, i)
                        link(dve.tensor_scalar(ld[:, :, :], cut(sgz, i), -0.6065306597126334, None, ALU.mult))
                        flat = [t[:, :, :].rearrange("p c n -> p (c n)") for t in (cum, ld)]
                        link(dve.tensor_tensor_scan(flat[0], starts[:, :], flat[1], 0.0, ALU.mult, ALU.add))
                        dve.tensor_tensor(eL[:, :, :], cum[:, :, :], ld[:, :, :], ALU.subtract).then_inc(r_cum, 1)

                    def unit(i):
                        dve.wait_ge(r_ss, i + 1)
                        dve.wait_ge(r_kr, i + 1)
                        dve.tensor_tensor(kk[:, :, :], kk[:, :, :], PS[:, 6, :].rearrange("p (c n) -> p c n", c=CT),
                                          ALU.mult).then_inc(r_rn, 1)
                        dve.wait_ge(r_rn, i + 1)

                    def keys(i):
                        if i >= 1:
                            dve.wait_ge(r_pP, i)
                        link(dve.scalar_tensor_tensor(kn[:, :, :], cut(sga, i), -1.0, by_c(3), ALU.add, ALU.mult))
                        dve.scalar_tensor_tensor(kn[:, :, :], kn[:, :, :], 1.0, cut(kT, i), ALU.add, ALU.mult).then_inc(r_kp, 1)

                    def beta(i):
                        link(dve.tensor_tensor(be[:, :, :], kk[:, :, :], cut(sga, i), ALU.mult))
                        dve.wait_ge(r_exp, 3 * i + 3)
                        link(dve.tensor_tensor(be[:, :, :], be[:, :, :], eN[:, :, :], ALU.mult))

                    def alpha(i):
                        dve.wait_ge(r_kp, i + 1)
                        link(dve.tensor_tensor(ka[:, :, :], kn[:, :, :], eN[:, :, :], ALU.mult))
                        dve.tensor_tensor(ar[:, i % 2, :, 0, :], kk[:, :, :], eL[:, :, :], ALU.mult).then_inc(r_pD, 1)

                    def seq(i, s):
                        q = i % 2
                        if s in (0, 3):
                            cp = s // 3
                            rows = slice(64 * cp, 64 * cp + 64)
                            dve.wait_ge(q_R, 2 * i + cp + 1)
                            dve.tensor_copy(Rb[rows, :], PS[rows, 4, :]).then_inc(q_Re, 1)
                        if s in (2, 5):
                            cp = s // 5
                            dve.wait_ge(q_S, 2 * i + cp + 1)
                            diag = [(slice(64 * a, 64 * a + 64), S[64 * a:64 * a + 64, :, 64 * a:64 * a + 64]) for a in range(2)]
                            for a, (rows, d) in enumerate(diag):
                                g = PS[rows, 6, :].rearrange("p (c n) -> p c n", c=CT)[:, :, 64 * a:64 * a + 64]
                                link(dve.tensor_tensor(d, d, g, ALU.add))
                            for rows, d in diag:
                                m = pc[rows, q, :, cp:cp + 1].to_broadcast([64, CT, 64])
                                dve.tensor_tensor(d, d, m, ALU.mult).then_inc(q_Se, 1)
                            dve.wait_ge(q_Se, 4 * i + 2 * cp + 2)

                    def post(i, s):
                        v = ysb[:, :].rearrange("p (h n) -> p h n", n=HD)

                        def per_head(a):
                            return a.unsqueeze(2).to_broadcast([P, NG, HD])
                        if s == 0:
                            dve.wait_ge(q_y1, i + 1)
                            link(dve.tensor_reduce(gn[:, 0, :], v, AX.X, ALU.add))
                            link(dve.tensor_scalar(gn[:, 0, :], gn[:, 0, :], 1.0 / HD, None, ALU.mult))
                            link(dve.tensor_tensor(v, v, per_head(gn[:, 0, :]), ALU.subtract))
                            link(dve.tensor_tensor(Sq[:, :, :], v, v, ALU.mult))
                            link(dve.tensor_reduce(gn[:, 1, :], Sq[:, :, :], AX.X, ALU.add))
                            link(dve.tensor_scalar(gn[:, 1, :], gn[:, 1, :], 1.0 / HD, GN_EPS, ALU.mult, ALU.add))
                            inverse_root(dve, link, gr[:, 0, :], gn[:, 1, :], gr[:, 1, :], gr[:, 2, :])
                            link(dve.tensor_tensor(v, v, per_head(gr[:, 0, :]), ALU.mult))
                        if s == 1:
                            link(dve.tensor_tensor(ysb[:, :], ysb[:, :], lng_b[:, :], ALU.mult))
                            link(dve.tensor_tensor(ysb[:, :], ysb[:, :], lnb_b[:, :], ALU.add))
                            dve.wait_ge(q_bg, i + 1)
                            link(dve.tensor_copy(gn[:, 2, :], PS[:, 6, 0:NG]))
                            link(dve.tensor_tensor(Sq[:, :, :].rearrange("p (c a) n -> p c a n", a=2),
                                                   cut(vT, i).rearrange("p c (a n) -> p c a n", a=2),
                                                   gn[:, 2, :].rearrange("p (c a) -> p c a", a=2).unsqueeze(3).to_broadcast([P, CT, 2, HD]),
                                                   ALU.mult))
                            link(dve.tensor_tensor(v, v, Sq[:, :, :], ALU.add))
                            dve.tensor_tensor(ysb[:, :], ysb[:, :], PS[:, 5, :], ALU.mult).then_inc(q_y2, 1)

                    decay(0)
                    unit(0)
                    keys(0)
                    beta(0)
                    alpha(0)
                    for i in range(NT):
                        q = i % 2
                        for n, dst in enumerate((BG, KG)):
                            for b in range(4):
                                dve.wait_ge(r_g, 8 * i + 4 * n + b + 1)
                                m = causal2[:, :, :].unsqueeze(1).to_broadcast([P, 2, 2, P])
                                dve.tensor_tensor(dst[:, q, 2 * b:2 * b + 2, :, :],
                                                  PS[:, b, :].rearrange("p (g a n) -> p g a n", g=2, a=2), m,
                                                  ALU.mult).then_inc(r_ge, 1)
                        dve.wait_ge(r_lm, NL * i + 1)
                        dve.tensor_tensor(XT[:, q, :, :], over_heads(ident[:, :], NG), LM[:, 0, :, :],
                                          ALU.subtract).then_inc(r_x0, 1)
                        more = i + 1 < NT
                        if more:
                            decay(i + 1)
                        for l in range(1, NL):
                            if i >= 1 and l <= 3:
                                seq(i - 1, 2 * l - 2)
                            if l == 1 and more:
                                unit(i + 1)
                            for hf in range(2):
                                dve.wait_ge(r_X, 2 * (NL - 1) * i + 2 * (l - 1) + hf + 1)
                                v = X[:, 4 * hf:4 * hf + 4, :]
                                dve.wait_ge(r_Te, 2 * NL * i + 2 + hf - 1)
                                dve.tensor_tensor(v, v, PS[:, 2 + hf, :].rearrange("p (c n) -> p c n", c=4),
                                                  ALU.subtract).then_inc(r_Xe, 1)
                            dve.wait_ge(r_Xe, 2 * (NL - 1) * i + 2 * l)
                            if i >= 1 and l <= 3:
                                seq(i - 1, 2 * l - 1)
                            if more and l == 2:
                                keys(i + 1)
                            if more and l == 3:
                                beta(i + 1)
                            if i >= 1 and l >= 4:
                                post(i - 1, l - 4)
                        if more:
                            alpha(i + 1)
                    for s in range(6):
                        seq(NT - 1, s)
                    post(NT - 1, 0)
                    post(NT - 1, 1)

        with ExitStack() as st:
            sbo = tile_in(st)
            wo = sbo("wo", [P, KT, D])
            g2b = sbo("g2b", [P, D])
            xo = sbo("xo", [P, 2, D])
            xn = sbo("xn", [P, 2, D])
            xn2T = sbo("xn2T", [P, KT, P])
            junk = sbo("junk", [P, D])
            rw = sbo("rw", [P, KT, NE])
            o_sq = sbo("o_sq", [P, NT])
            o_rs = sbo("o_rs", [P, 4, NT])
            lg = sbo("lg", [P, NT, NE])
            v8 = sbo("v8", [P, NT, 8])
            i8 = sbo("i8", [P, NT, 8], u32)
            ix4 = sbo("ix4", [P, NT, TOPK])
            OH = sbo("OH", [P, NT * TOPK, NE])
            pick = sbo("pick", [P, NT, NE])
            past = sbo("past", [P, NT + 1, NE])
            sv = sbo("sv", [P, NT, NE])
            e_io = sbo("e_io", [P, NE])
            p_io = sbo("p_io", [P, 1])
            ioi = sbo("ioi", [P, NE + 1], i32)
            cnt, nit, inc, base, tmp, first = (sbo(n, [P, NE]) for n in ("cnt", "nit", "inc", "base", "tmp", "first"))
            it = sbo("it", [P, 8])
            itab = sbo("itab", [P, 4], i32)
            gsum = sbo("gsum", [P, NT, 1])
            sf = sbo("sf", [P, NT * TOPK])
            tokid = sbo("tokid", [P, NT], u32)
            o_w, o_x, o_mm, o_h, o_ssq, o_xn, o_hd, o_xd = (sem(n) for n in ("o_w", "o_x", "o_mm", "o_h", "o_ssq", "o_xn", "o_hd", "o_xd"))
            o_xs = (sem("o_xs0"), sem("o_xs1"))
            o_t, o_te, o_lg, o_le, o_dc, o_pc, o_io = (sem(n) for n in ("o_t", "o_te", "o_lg", "o_le", "o_dc", "o_pc", "o_io"))
            o_pk, o_rk, o_dv, o_ex, o_sl, o_it, o_sc, o_itd = (sem(n) for n in ("o_pk", "o_rk", "o_dv", "o_ex", "o_sl", "o_it", "o_sc", "o_itd"))
            o_hds = (sem("o_hd0"), sem("o_hd1"))
            o_xds = (sem("o_xd0"), sem("o_xd1"))
            h_rows = h_d.rearrange("(j p) d -> j p d", p=P)
            xn_rows = xn2_d.rearrange("(j p) d -> j p d", p=P)
            with nc.Block() as block:
                @block.sync
                def _(sp):
                    sp.dma_start(big[:, 0:CT, :], att_d).then_inc(o_w, 16)
                    sp.dma_start(wo[:, :, :], A["w_out"][0].rearrange("(k p) n -> p k n", p=P)).then_inc(o_w, 16)
                    sp.dma_start(g2b[:, :], A["norm2_g"][0].partition_broadcast(P)).then_inc(o_w, 16)
                    sp.dma_start(rw[:, :, :], A["router_w"][0].rearrange("(k p) n -> p k n", p=P)).then_inc(o_w, 16)
                    for j in range(2):
                        sp.dma_start(xo[:, j, :], x_rows[j]).then_inc(o_xs[j], 16)
                    for j in range(NT):
                        sp.wait_ge(o_h, j + 1)
                        sp.dma_start(h_rows[j], xo[:, j % 2, :]).then_inc(o_hds[j % 2], 16)
                        sp.wait_ge(o_xn, j + 1)
                        sp.dma_start(xn_rows[j], xn[:, j % 2, :]).then_inc(o_xds[j % 2], 16)
                        if j + 2 < NT:
                            sp.wait_ge(o_hds[j % 2], 16 * (j // 2 + 1))
                            sp.dma_start(xo[:, j % 2, :], x_rows[j + 2]).then_inc(o_xs[j % 2], 16)
                    sp.wait_ge(o_it, 1)
                    sp.dma_start(item_d, itab[:, :]).then_inc(o_itd, 16)
                    sp.wait_ge(o_itd, 16)
                    for a in range(2):
                        sp.wait_ge(o_hds[a], 16 * NT // 2)
                        sp.wait_ge(o_xds[a], 16 * NT // 2)
                    sp.wait_ge(o_sc, 16 * NT * TOPK)

                @block.tensor
                def _(pe):
                    pe.wait_ge(o_w, 64)

                    def project(j):
                        if j >= 2:
                            pe.wait_ge(o_h, j - 1)
                        for th in range(2):
                            for k in range(KT):
                                src = rT if k < CT else big
                                ins = pe.matmul(PS[:, 2 * (j % 2) + th, :], src[:, k % CT, j * P:(j + 1) * P],
                                                wo[:, k, th * 512:(th + 1) * 512], start=(k == 0), stop=(k == KT - 1))
                        ins.then_inc(o_mm, 1)

                    def route(j):
                        pe.wait_ge(o_xn, j + 1)
                        if j >= 1:
                            pe.wait_ge(o_te, j)
                        for k in range(KT):
                            ins = pe.transpose(PS[:, 4 + k // 4, (k % 4) * P:(k % 4 + 1) * P],
                                               xn[:, j % 2, k * P:(k + 1) * P], ident[:, :])
                        ins.then_inc(o_t, 1)
                        pe.wait_ge(o_te, j + 1)
                        if j >= 2:
                            pe.wait_ge(o_le, j - 1)
                        for k in range(KT):
                            ins = pe.matmul(PS[:, 6 + j % 2, 0:NE], xn2T[:, k, :], rw[:, k, :],
                                            start=(k == 0), stop=(k == KT - 1))
                        ins.then_inc(o_lg, 1)

                    project(0)
                    for j in range(NT):
                        if j + 1 < NT:
                            project(j + 1)
                        route(j)
                    pe.wait_ge(o_pk, 1)
                    pe.matmul(PS[:, 0, 0:NT * NE], later[:, :], pick[:, :, :].rearrange("p t e -> p (t e)"),
                              start=True, stop=False)
                    pe.matmul(PS[:, 0, 0:NT * NE], ones[:, :], past[:, 0:NT, :].rearrange("p t e -> p (t e)"),
                              start=False, stop=True)
                    pe.matmul(PS[:, 2, 0:NE], ones[:, :], past[:, NT, :], start=True, stop=True).then_inc(o_rk, 1)

                @block.scalar
                def _(act):
                    for j in range(NT):
                        act.wait_ge(o_h, j + 1)
                        act.activation(junk[:, :], xo[:, j % 2, :], ACT.Square,
                                       accum_out=o_sq[:, j:j + 1]).then_inc(o_ssq, 1)
                        act.wait_ge(o_ssq, j + 1)
                        act.wait_ge(o_t, j + 1)
                        act.activation(xn2T[:, :, :].rearrange("p k n -> p (k n)"), pair(2), ACT.Copy).then_inc(o_te, 1)
                    act.wait_ge(o_dv, 1)
                    act.activation(gates[:, :, :], gates[:, :, :], ACT.Exp).then_inc(o_ex, 1)

                @block.gpsimd
                def _(pool):
                    link = linker(pool, o_pc)
                    link(pool.iota(ioi[:, 0:NE], [[1, NE]], base=0, channel_multiplier=0))
                    link(pool.iota(ioi[:, NE:NE + 1], [[0, 1]], base=0, channel_multiplier=1))
                    link(pool.iota(tokid[:, :], [[P, NT]], base=0, channel_multiplier=1))
                    link(pool.tensor_copy(e_io[:, :], ioi[:, 0:NE]))
                    link(pool.tensor_copy(p_io[:, :], ioi[:, NE:NE + 1]))
                    pool.sem_inc(o_io, 1)
                    pool.wait_ge(o_sl, 1)
                    for n in range(NT * TOPK):
                        pool.indirect_dma_start(slot_d[:, :], bass.IndirectOffsetOnAxis(slots_u[:, n:n + 1], 0),
                                                tokid[:, n // TOPK:n // TOPK + 1], None).then_inc(o_sc, 16)

                @block.vector
                def _(dve):
                    link = linker(dve, o_dc)

                    def logits(j):
                        dve.wait_ge(o_lg, j + 1)
                        dve.tensor_tensor(lg[:, j, :], PS[:, 6 + j % 2, 0:NE], rb_b[:, :], ALU.add).then_inc(o_le, 1)
                        dve.wait_ge(o_le, j + 1)
                        link(dve.max(v8[:, j, :], lg[:, j, :]))
                        link(dve.max_index(i8[:, j, :], v8[:, j, :], lg[:, j, :]))

                    for j in range(NT):
                        dve.wait_ge(o_mm, j + 1)
                        dve.wait_ge(o_xs[j % 2], 16 * (j // 2 + 1))
                        dve.tensor_tensor(xo[:, j % 2, :], xo[:, j % 2, :], pair(j % 2), ALU.add).then_inc(o_h, 1)
                        dve.wait_ge(o_ssq, j + 1)
                        r = [o_rs[:, n, j:j + 1] for n in range(4)]
                        link(dve.tensor_scalar(r[1], o_sq[:, j:j + 1], 1.0 / D, NORM_EPS, ALU.mult, ALU.add))
                        inverse_root(dve, link, *r)
                        if j >= 2:
                            dve.wait_ge(o_xds[j % 2], 16 * (j // 2))
                            dve.wait_ge(o_t, j - 1)
                        dve.scalar_tensor_tensor(xn[:, j % 2, :], xo[:, j % 2, :], r[0], g2b[:, :],
                                                 ALU.mult, ALU.mult).then_inc(o_xn, 1)
                        if j >= 1:
                            logits(j - 1)
                    logits(NT - 1)
                    link(dve.tensor_tensor(gates[:, :, :], v8[:, :, 0:TOPK], v8[:, :, 0:1].to_broadcast([P, NT, TOPK]),
                                           ALU.subtract))
                    dve.sem_inc(o_dv, 1)
                    dve.wait_ge(o_io, 1)
                    link(dve.tensor_copy(ix4[:, :, :], i8[:, :, 0:TOPK]))
                    link(dve.tensor_tensor(OH[:, :, :], e_io[:, :].unsqueeze(1).to_broadcast([P, NT * TOPK, NE]),
                                           ix4[:, :, :].rearrange("p t k -> p (t k)").unsqueeze(2).to_broadcast([P, NT * TOPK, NE]),
                                           ALU.is_equal))
                    link(dve.tensor_reduce(pick[:, :, :], OH[:, :, :].rearrange("p (t k) e -> p t e k", k=TOPK), AX.X, ALU.add))
                    link(dve.memset(past[:, 0, :], 0.0))
                    for j in range(NT):
                        link(dve.tensor_tensor(past[:, j + 1, :], past[:, j, :], pick[:, j, :], ALU.add))
                    dve.sem_inc(o_pk, 1)
                    dve.wait_ge(o_rk, 1)
                    link(dve.tensor_copy(cnt[:, :], PS[:, 2, 0:NE]))
                    link(dve.tensor_scalar(nit[:, :], cnt[:, :], 0.0, None, ALU.is_gt))
                    for m in range(1, T // SLOTS):
                        link(dve.scalar_tensor_tensor(nit[:, :], cnt[:, :], float(SLOTS * m), nit[:, :], ALU.is_gt, ALU.add))
                    link(dve.tensor_tensor_scan(inc[:, :], ones[:, 0:NE], nit[:, :], 0.0, ALU.mult, ALU.add))
                    link(dve.tensor_tensor(base[:, :], inc[:, :], nit[:, :], ALU.subtract))
                    link(dve.tensor_scalar(base[:, :], base[:, :], float(SLOTS), None, ALU.mult))
                    link(dve.tensor_tensor_scan(first[:, :], ones[:, 0:NE], cnt[:, :], 0.0, ALU.mult, ALU.add))
                    link(dve.tensor_tensor(first[:, :], first[:, :], cnt[:, :], ALU.subtract))
                    link(dve.tensor_tensor(sv[:, :, :], PS[:, 0, 0:NT * NE].rearrange("p (t e) -> p t e", e=NE),
                                           first[:, :].unsqueeze(1).to_broadcast([P, NT, NE]), ALU.add))
                    v4 = OH[:, :, :].rearrange("p (t k) e -> p t k e", k=TOPK)
                    link(dve.tensor_tensor(v4, v4, sv[:, :, :].unsqueeze(2).to_broadcast([P, NT, TOPK, NE]), ALU.mult))
                    link(dve.tensor_reduce(sf[:, :], OH[:, :, :], AX.X, ALU.add))
                    link(dve.tensor_copy(slots_u[:, :], sf[:, :]))
                    dve.sem_inc(o_sl, 1)
                    link(dve.tensor_scalar(tmp[:, :], inc[:, :], p_io[:, 0:1], None, ALU.is_le))
                    link(dve.tensor_reduce(it[:, 0:1], tmp[:, :], AX.X, ALU.add))
                    link(dve.tensor_scalar(it[:, 0:1], it[:, 0:1], float(NE - 1), None, ALU.min))
                    link(dve.tensor_scalar(tmp[:, :], e_io[:, :], it[:, 0:1], None, ALU.is_equal))
                    link(dve.tensor_tensor(cnt[:, :], cnt[:, :], base[:, :], ALU.add))
                    link(dve.tensor_tensor(first[:, :], first[:, :], base[:, :], ALU.subtract))
                    link(dve.tensor_tensor(first[:, :], tmp[:, :], first[:, :], ALU.mult))
                    link(dve.tensor_reduce(it[:, 5:6], first[:, :], AX.X, ALU.add))
                    link(dve.tensor_tensor(tmp[:, :], tmp[:, :], cnt[:, :], ALU.mult))
                    link(dve.tensor_reduce(it[:, 3:4], tmp[:, :], AX.X, ALU.add))
                    link(dve.scalar_tensor_tensor(it[:, 4:5], p_io[:, :], -float(SLOTS), it[:, 3:4], ALU.mult, ALU.add))
                    link(dve.tensor_scalar(it[:, 1:2], it[:, 4:5], float(P), None, ALU.is_gt))
                    link(dve.tensor_copy(it[:, 2:3], inc[:, NE - 1:NE]))
                    link(dve.scalar_tensor_tensor(it[:, 3:4], p_io[:, :], float(SLOTS), it[:, 5:6], ALU.mult, ALU.add))
                    link(dve.tensor_scalar(it[:, 3:4], it[:, 3:4], float(T * TOPK), None, ALU.min))
                    link(dve.tensor_copy(itab[:, :], it[:, 0:4]))
                    dve.sem_inc(o_it, 1)
                    dve.wait_ge(o_ex, 1)
                    link(dve.tensor_reduce(gsum[:, :, :], gates[:, :, :], AX.X, ALU.add))
                    link(dve.reciprocal(gsum[:, :, :], gsum[:, :, :]))
                    link(dve.tensor_tensor(gates[:, :, :], gates[:, :, :], gsum[:, :, :].to_broadcast([P, NT, TOPK]), ALU.mult))
        mix.close()
        small.close()

        UNITS, KH = 12, KT // 2
        NRAW, NSPL = 4, 6
        with ExitStack() as st:
            sbe = tile_in(st)
            raw = sbe("raw", [P, NRAW, KH, 512])
            wh = sbe("wh", [P, NSPL, KH, 512], f32r)
            wl = sbe("wl", [P, NSPL, KH, 512], f32r)
            xh = sbe("xh", [P, KT, SLOTS], f32r)
            xl = sbe("xl", [P, KT, SLOTS], f32r)
            ah = sbe("ah", [P, KT, SLOTS], f32r)
            al = sbe("al", [P, KT, SLOTS], f32r)
            xg = sbe("xg", [P, 2, D])
            hb = sbe("hb", [P, 2, 512])
            gl = sbe("gl", [P, 2, 256])
            li = sbe("li", [P, 2, 256])
            sg = sbe("sg", [P, 2, 256])
            av = sbe("av", [P, 2, 2, 256])
            yb = sbe("yb", [P, 2, D])
            bu = sbe("bu", [P, 2 * D])
            bd = sbe("bd", [P, D])
            idx = sbe("idx", [P, 2], u32)
            items_t = sbe("items_t", [1, (MAXI + 2) * 4], i32)
            e_raw = [sem(f"e_raw{n}") for n in range(NRAW)]
            e_hi, e_lo, e_used = sem("e_hi"), sem("e_lo"), sem("e_used")
            e_up, e_bank, e_gl, e_sg, e_av, e_T, e_ah, e_al = (sem(n) for n in ("e_up", "e_bank", "e_gl", "e_sg", "e_av", "e_T", "e_ah", "e_al"))
            e_X, e_xh, e_xl, e_dn, e_y, e_yd, e_ix, e_gt, e_rowu, e_rowd, e_bu, e_bd = (sem(n) for n in ("e_X", "e_xh", "e_xl", "e_dn", "e_y", "e_yd", "e_ix", "e_gt", "e_rowu", "e_rowd", "e_bu", "e_bd"))
            e_pw, e_tw, e_tab = sem("e_pw"), sem("e_tw"), sem("e_tab")
            w_up = A["exp_w_up"][0].rearrange("e (k p) n -> e p k n", p=P)
            w_dn = A["exp_w_down"][0].rearrange("e (k p) n -> e p k n", p=P)

            def field(eng, i, n, lo, hi):
                return eng.value_load(items_t[0:1, bass.ds(4 * i + n, 1)], min_val=lo, max_val=hi)

            def items(eng):
                return eng.value_load(items_t[0:1, 2:3], min_val=1, max_val=MAXI)

            def expert(eng, i):
                return field(eng, i, 0, 0, NE - 1)

            def first_slot(eng, i):
                return field(eng, i, 3, 0, T * TOPK)

            def by_blocks(eng, i, body):
                two = field(eng, i, 1, 0, 1)
                with eng.If(two > 0):
                    body(2)
                with eng.Else():
                    body(1)

            with nc.Block() as block:
                @block.sync
                def _(sp):
                    def load(e, u, g, wait=True):
                        if wait:
                            sp.wait_ge(e_lo, g - (NRAW - 1))
                        if u < 8:
                            src = w_up[bass.ds(e, 1), :, (u % 2) * KH:(u % 2 + 1) * KH, (u // 2) * 512:(u // 2 + 1) * 512]
                        else:
                            d, kh = (u - 8) % 2, (u - 8) // 2
                            src = w_dn[bass.ds(e, 1), :, kh * KH:(kh + 1) * KH, d * 512:(d + 1) * 512]
                        sp.dma_start(raw[:, u % NRAW, :, :], src.rearrange("a p k n -> (a p) k n")).then_inc(e_raw[u % NRAW], 16)

                    sp.dma_start(items_t[0:1, :], item_d[0:MAXI + 2, :].rearrange("p n -> (p n)").unsqueeze(0)).then_inc(e_tab, 16)
                    sp.wait_ge(e_tab, 16)
                    e0 = expert(sp, 0)
                    for u in range(NSPL):
                        load(e0, u, u, wait=(u >= NRAW))
                    with sp.Fori(0, items(sp)) as i:
                        e = expert(sp, i)
                        for u in range(NSPL, UNITS):
                            load(e, u, UNITS * i + u)
                        en = expert(sp, i + 1)
                        for u in range(NSPL):
                            load(en, u, UNITS * (i + 1) + u)

                @block.tensor
                def _(pe):
                    def unit(i, nb, u):
                        pe.wait_ge(e_lo, UNITS * i + u + 1)
                        if u < 8:
                            s, kh = u // 2, u % 2
                            use, left, bank = s, (xh, xl), 2 * (s % 2)
                            if u == 0:
                                pe.wait_ge(e_xl, 4 * i + 4)
                        else:
                            d, kh = (u - 8) % 2, (u - 8) // 2
                            use, left, bank = 4 + d, (ah, al), 2 * d
                            pe.wait_ge(e_al, 4 * i + 2 + 2 + 2 * kh)
                        if kh == 0:
                            pe.wait_ge(e_bank, 6 * i + use + 1)
                        for b in range(nb):
                            for n in range(KH):
                                k = kh * KH + n
                                for m, (x_, w_) in enumerate(((0, 0), (0, 1), (1, 0))):
                                    ins = pe.matmul(PS[:, bank + b, :], left[x_][:, k, b * P:(b + 1) * P],
                                                    (wh, wl)[w_][:, u % NSPL, n, :],
                                                    start=(k == 0 and m == 0), stop=(k == KT - 1 and m == 2))
                        ins.then_inc(e_used, 1)

                    def flip_x(i, x):
                        pe.wait_ge(e_gt, 32 * (i + 1))
                        pe.wait_ge(e_xl, 4 * i + x - 1)
                        for n in range(4):
                            k = (x % 2) * 4 + n
                            ins = pe.transpose(PS[:, 6 + x % 2, n * P:(n + 1) * P], xg[:, x // 2, k * P:(k + 1) * P], ident[:, :])
                        ins.then_inc(e_X, 1)

                    def flip_a(i, nb, s):
                        pe.wait_ge(e_av, 4 * i + s + 1)
                        pe.wait_ge(e_al, 4 * i + s + 1)
                        for b in range(nb):
                            for n in range(2):
                                ins = pe.transpose(PS[:, 4 + s % 2, (2 * b + n) * P:(2 * b + n + 1) * P],
                                                   av[:, s % 2, b, n * P:(n + 1) * P], ident[:, :])
                        ins.then_inc(e_T, 1)

                    for x in range(4):
                        pe.wait_ge(e_gt, 32)
                        if x >= 2:
                            pe.wait_ge(e_xl, x - 1)
                        for n in range(4):
                            k = (x % 2) * 4 + n
                            ins = pe.transpose(PS[:, 6 + x % 2, n * P:(n + 1) * P], xg[:, x // 2, k * P:(k + 1) * P], ident[:, :])
                        ins.then_inc(e_X, 1)
                    pe.wait_ge(e_tab, 16)
                    with pe.Fori(0, items(pe)) as i:
                        def body(nb):
                            for s in range(4):
                                unit(i, nb, 2 * s)
                                unit(i, nb, 2 * s + 1)
                                if s >= 1:
                                    flip_a(i, nb, s - 1)
                            unit(i, nb, 8)
                            flip_x(i + 1, 0)
                            flip_x(i + 1, 1)
                            unit(i, nb, 9)
                            flip_a(i, nb, 3)
                            flip_x(i + 1, 2)
                            flip_x(i + 1, 3)
                            unit(i, nb, 10)
                            unit(i, nb, 11)
                        by_blocks(pe, i, body)

                @block.scalar
                def _(act):
                    def head(i, u, wait=True):
                        act.wait_ge(e_raw[u % NRAW], 16 * ((UNITS // NRAW) * i + u // NRAW + 1))
                        if wait:
                            act.wait_ge(e_used, UNITS * i + u - (NSPL - 1))
                        act.activation(wh[:, u % NSPL, :, :], raw[:, u % NRAW, :, :], ACT.Copy).then_inc(e_hi, 1)

                    def x_head(i, x):
                        act.wait_ge(e_X, 4 * i + x + 1)
                        act.activation(xh[:, (x % 2) * 4:(x % 2) * 4 + 4, (x // 2) * P:(x // 2 + 1) * P],
                                       PS[:, 6 + x % 2, :].rearrange("p (k n) -> p k n", k=4), ACT.Copy).then_inc(e_xh, 1)

                    def a_head(i, nb, s):
                        act.wait_ge(e_T, 4 * i + s + 1 + 2)
                        act.activation(ah[:, 2 * s:2 * s + 2, 0:nb * P].rearrange("p k (b n) -> p b k n", b=nb),
                                       PS[:, 4 + s % 2, 0:nb * 256].rearrange("p (b k n) -> p b k n", b=nb, k=2),
                                       ACT.Copy).then_inc(e_ah, 1)

                    def sigmoid(i, nb, s):
                        act.wait_ge(e_gl, 8 * i + 2 * s + 1)
                        act.activation(sg[:, 0:nb, :], gl[:, 0:nb, :], ACT.Sigmoid, scale=1.702).then_inc(e_sg, 1)

                    for x in range(4):
                        x_head(0, x)
                    for u in range(NSPL):
                        head(0, u, wait=False)
                    act.wait_ge(e_tab, 16)
                    with act.Fori(0, items(act)) as i:
                        def body(nb):
                            for s in range(4):
                                head(i, 2 * s + NSPL) if s < 3 else head(i + 1, 0)
                                head(i, 2 * s + NSPL + 1) if s < 3 else head(i + 1, 1)
                                if s >= 1:
                                    a_head(i, nb, s - 1)
                                sigmoid(i, nb, s)
                            x_head(i + 1, 0)
                            x_head(i + 1, 1)
                            head(i + 1, 2)
                            a_head(i, nb, 3)
                            x_head(i + 1, 2)
                            x_head(i + 1, 3)
                            head(i + 1, 3)
                            head(i + 1, 4)
                            head(i + 1, 5)
                        by_blocks(act, i, body)

                @block.vector
                def _(dve):
                    def rest(i, u):
                        dve.wait_ge(e_hi, UNITS * i + u + 1)
                        dve.tensor_tensor(wl[:, u % NSPL, :, :], raw[:, u % NRAW, :, :],
                                          wh[:, u % NSPL, :, :].bitcast(f32), ALU.subtract).then_inc(e_lo, 1)

                    def x_rest(i, x):
                        dve.wait_ge(e_xh, 4 * i + x + 1)
                        cut_ = (slice(None), slice((x % 2) * 4, (x % 2) * 4 + 4), slice((x // 2) * P, (x // 2 + 1) * P))
                        dve.tensor_tensor(xl[cut_], PS[:, 6 + x % 2, :].rearrange("p (k n) -> p k n", k=4),
                                          xh[cut_].bitcast(f32), ALU.subtract).then_inc(e_xl, 1)

                    def a_rest(i, nb, s):
                        dve.wait_ge(e_ah, 4 * i + s + 1)
                        out_, in_ = (t[:, 2 * s:2 * s + 2, 0:nb * P].rearrange("p k (b n) -> p b k n", b=nb) for t in (al, ah))
                        dve.tensor_tensor(out_, PS[:, 4 + s % 2, 0:nb * 256].rearrange("p (b k n) -> p b k n", b=nb, k=2),
                                          in_.bitcast(f32), ALU.subtract).then_inc(e_al, 1)

                    def add_up(i, nb, s):
                        dve.wait_ge(e_used, UNITS * i + 2 * s + 2)
                        dve.wait_ge(e_bu, i + 1)
                        dve.tensor_tensor(hb[:, 0:nb, :], PS[:, 2 * (s % 2):2 * (s % 2) + nb, :],
                                          bu[:, s * 512:(s + 1) * 512].unsqueeze(1).to_broadcast([P, nb, 512]),
                                          ALU.add).then_inc(e_bank, 1)

                    def glu(i, nb, s):
                        dve.wait_ge(e_gl, 8 * i + 2 * s + 2)
                        dve.wait_ge(e_T, 4 * i + s + 1)
                        dve.scalar_tensor_tensor(hb[:, 0:nb, 0:256], li[:, 0:nb, :], 1.0, gl[:, 0:nb, :],
                                                 ALU.add, ALU.mult).then_inc(e_tw, 1)
                        dve.wait_ge(e_tw, 4 * i + s + 1)
                        dve.wait_ge(e_sg, 4 * i + s + 1)
                        dve.tensor_tensor(av[:, s % 2, 0:nb, :], hb[:, 0:nb, 0:256], sg[:, 0:nb, :], ALU.mult).then_inc(e_av, 1)
                        dve.wait_ge(e_av, 4 * i + s + 1)

                    def add_dn(i, nb, d):
                        dve.wait_ge(e_used, UNITS * i + 11 + d)
                        dve.wait_ge(e_bd, i + 1)
                        if d == 0:
                            dve.wait_ge(e_yd, 16 * i + 16)
                        dve.tensor_tensor(yb[:, 0:nb, d * 512:(d + 1) * 512], PS[:, 2 * d:2 * d + nb, :],
                                          bd[:, d * 512:(d + 1) * 512].unsqueeze(1).to_broadcast([P, nb, 512]),
                                          ALU.add).then_inc(e_bank, 1)

                    dve.sem_inc(e_bank, 2)
                    dve.sem_inc(e_al, 2)
                    dve.sem_inc(e_T, 2)
                    for x in range(4):
                        x_rest(0, x)
                    for u in range(NSPL):
                        rest(0, u)
                    dve.wait_ge(e_tab, 16)
                    with dve.Fori(0, items(dve)) as i:
                        def body(nb):
                            for s in range(4):
                                rest(i, 2 * s + NSPL) if s < 3 else rest(i + 1, 0)
                                add_up(i, nb, s)
                                if s >= 1:
                                    a_rest(i, nb, s - 1)
                                rest(i, 2 * s + NSPL + 1) if s < 3 else rest(i + 1, 1)
                                glu(i, nb, s)
                            x_rest(i + 1, 0)
                            x_rest(i + 1, 1)
                            rest(i + 1, 2)
                            a_rest(i, nb, 3)
                            x_rest(i + 1, 2)
                            x_rest(i + 1, 3)
                            rest(i + 1, 3)
                            add_dn(i, nb, 0)
                            rest(i + 1, 4)
                            add_dn(i, nb, 1)
                            rest(i + 1, 5)
                        by_blocks(dve, i, body)

                @block.gpsimd
                def _(pool):
                    def hold(counter, value):
                        pool.wait_ge(counter, value)
                        pool.sem_inc(e_pw, 1)

                    def gather(i):
                        for b in range(2):
                            pool.indirect_dma_start(xg[:, b, :], None, xn2_d[:, :],
                                                    bass.IndirectOffsetOnAxis(idx[:, b:b + 1], 0)).then_inc(e_gt, 16)

                    def indices(i):
                        src = slot_d[bass.ds(first_slot(pool, i), SLOTS), :].rearrange("(b p) a -> p (b a)", p=P)
                        with nc.allow_non_contiguous_dma(reason="token indices, 1 KiB"):
                            pool.dma_start(idx[:, :], src).then_inc(e_ix, 16)

                    def bias(e, row, dst, done):
                        pool.dma_start(dst[0:1, :], row[bass.ds(e, 1), :]).then_inc(done, 16)

                    def clamp(i, nb, s):
                        hold(e_bank, 6 * i + s + 3)
                        v = hb[:, 0:nb, :].rearrange("p b (n a) -> p b n a", a=2)
                        pool.tensor_scalar(gl[:, 0:nb, :], v[:, :, :, 0], 7.0, None, ALU.min).then_inc(e_gl, 1)
                        pool.tensor_scalar(li[:, 0:nb, :], v[:, :, :, 1], 7.0, -7.0, ALU.min, ALU.max).then_inc(e_gl, 1)

                    pool.wait_ge(e_tab, 16)
                    e0 = expert(pool, 0)
                    indices(0)
                    pool.wait_ge(e_ix, 16)
                    gather(0)
                    pool.dma_start(pad_d, idx[:, :]).then_inc(e_yd, 16)
                    bias(e0, A["exp_b_up"][0], bu, e_rowu)
                    pool.wait_ge(e_rowu, 16)
                    pool.partition_broadcast(bu[:, :], bu[0:1, :]).then_inc(e_bu, 1)
                    pool.wait_ge(e_gt, 32)
                    indices(1)
                    pool.wait_ge(e_X, 4)
                    with pool.Fori(0, items(pool)) as i:
                        e, en = expert(pool, i), expert(pool, i + 1)

                        def body(nb):
                            clamp(i, nb, 0)
                            bias(e, A["exp_b_down"][0], bd, e_rowd)
                            hold(e_X, 4 * i + 4)
                            hold(e_ix, 16 * i + 32)
                            gather(i + 1)
                            clamp(i, nb, 1)
                            hold(e_rowd, 16 * i + 16)
                            pool.partition_broadcast(bd[:, :], bd[0:1, :]).then_inc(e_bd, 1)
                            clamp(i, nb, 2)
                            clamp(i, nb, 3)
                            bias(en, A["exp_b_up"][0], bu, e_rowu)
                            hold(e_gt, 32 * i + 64)
                            indices(i + 2)
                            hold(e_rowu, 16 * i + 32)
                            pool.partition_broadcast(bu[:, :], bu[0:1, :]).then_inc(e_bu, 1)
                            hold(e_bank, 6 * i + 8)
                            rows = ys_d[bass.ds(first_slot(pool, i), nb * P), :].rearrange("(b p) d -> p b d", p=P)
                            pool.dma_start(rows, yb[:, 0:nb, :]).then_inc(e_yd, 16)
                        by_blocks(pool, i, body)
                    hold(e_yd, 16 * items(pool) + 16)
                    pool.wait_ge(e_ix, 32)

        with ExitStack() as st:
            sbc = tile_in(st)
            yg = sbc("yg", [P, 2, TOPK, D])
            hh = sbc("hh", [P, 2, D])
            fgb = sbc("fgb", [P, D])
            cj = sbc("cj", [P, D])
            c_sq = sbc("c_sq", [P, NT])
            c_rs = sbc("c_rs", [P, 4, NT])
            c_g, c_h, c_o = ((sem(f"{n}0"), sem(f"{n}1")) for n in ("c_g", "c_h", "c_o"))
            c_f, c_dc, c_a, c_s, c_n = (sem(n) for n in ("c_f", "c_dc", "c_a", "c_s", "c_n"))
            out_rows = out[0].rearrange("(j p) d -> j p d", p=P)
            with nc.Block() as block:
                @block.sync
                def _(sp):
                    sp.dma_start(fgb[:, :], A["final_g"].partition_broadcast(P)).then_inc(c_f, 16)
                    for j in range(2):
                        sp.dma_start(hh[:, j, :], h_rows[j]).then_inc(c_h[j], 16)
                    for j in range(NT):
                        sp.wait_ge(c_n, j + 1)
                        sp.dma_start(out_rows[j], hh[:, j % 2, :]).then_inc(c_o[j % 2], 16)
                        if j + 2 < NT:
                            sp.wait_ge(c_o[j % 2], 16 * (j // 2 + 1))
                            sp.dma_start(hh[:, j % 2, :], h_rows[j + 2]).then_inc(c_h[j % 2], 16)
                    for a in range(2):
                        sp.wait_ge(c_o[a], 16 * NT // 2)

                @block.gpsimd
                def _(pool):
                    for j in range(NT):
                        if j >= 2:
                            pool.wait_ge(c_a, j - 1)
                        for k in range(TOPK):
                            n = j * TOPK + k
                            pool.indirect_dma_start(yg[:, j % 2, k, :], None, ys_d[0:T * TOPK, :],
                                                    bass.IndirectOffsetOnAxis(slots_u[:, n:n + 1], 0)).then_inc(c_g[j % 2], 16)

                @block.vector
                def _(dve):
                    link = linker(dve, c_dc)
                    dve.wait_ge(c_f, 16)
                    for j in range(NT):
                        h = hh[:, j % 2, :]
                        dve.wait_ge(c_h[j % 2], 16 * (j // 2 + 1))
                        dve.wait_ge(c_g[j % 2], 16 * TOPK * (j // 2 + 1))
                        for k in range(TOPK):
                            ins = dve.scalar_tensor_tensor(h, yg[:, j % 2, k, :], gates[:, j, k:k + 1], h, ALU.mult, ALU.add)
                            if k + 1 < TOPK:
                                link(ins)
                        ins.then_inc(c_a, 1)
                        dve.wait_ge(c_s, j + 1)
                        r = [c_rs[:, n, j:j + 1] for n in range(4)]
                        link(dve.tensor_scalar(r[1], c_sq[:, j:j + 1], 1.0 / D, NORM_EPS, ALU.mult, ALU.add))
                        inverse_root(dve, link, *r)
                        dve.scalar_tensor_tensor(h, h, r[0], fgb[:, :], ALU.mult, ALU.mult).then_inc(c_n, 1)

                @block.scalar
                def _(act):
                    for j in range(NT):
                        act.wait_ge(c_a, j + 1)
                        act.activation(cj[:, :], hh[:, j % 2, :], ACT.Square, accum_out=c_sq[:, j:j + 1]).then_inc(c_s, 1)
                        act.wait_ge(c_s, j + 1)


_OUTS = [((1, 1024, 1024), 'float32')]


def kernel(**inputs):
    import numpy as _np
    import concourse.bacc as _bacc
    from concourse import mybir as _mybir
    from concourse.bass_utils import run_bass_kernel_spmd as _run

    nc = _bacc.Bacc("TRN2", target_bir_lowering=False, num_devices=1)
    arrays, args = {}, {}
    for name in inputs:
        a = _np.ascontiguousarray(inputs[name])
        arrays[f"in_{name}_dram"] = a
        args[name] = nc.dram_tensor(f"in_{name}_dram", a.shape, _mybir.dt.from_np(a.dtype), kind="ExternalInput").ap()
    shape, dtype = _OUTS[0]
    out = nc.dram_tensor("out_0_dram", shape, _mybir.dt.from_np(_np.dtype(dtype)), kind="ExternalOutput").ap()
    layer_program(nc, args, out)
    r = _run(nc, [arrays], core_ids=[0])
    return r.results[0]["out_0_dram"]
```

```python
import concourse.bass as bass
from concourse import mybir
from contextlib import ExitStack

P = 128
D = 1024
T = 1024
NT = T // P
KT = D // P
W = 512
CT = W // P
HD = 64
NG = W // HD
NE = 32
TOPK = 4
SLOTS = 2 * P
NSLOT = T * TOPK + SLOTS
MAXI = T * TOPK // SLOTS + NE
LEVELS = [1, 2, 4, 8, 16, 32]
NEG = -1.0e30
LAMBDA_INIT = 0.2
NORM_EPS = 1e-5
GN_EPS = 64e-5


def linker(eng, own):
    def link(ins):
        own[1] += 1
        ins.then_inc(own[0], 1)
        eng.wait_ge(own[0], own[1])
    return link


def inverse_root(dve, link, y, x, t, half):
    i32, ALU = mybir.dt.int32, mybir.AluOpType
    link(dve.tensor_scalar(half, x, -0.5, None, ALU.mult))
    link(dve.tensor_scalar(y.bitcast(i32), x.bitcast(i32), -0.5, float(0x5F3759DF), ALU.mult, ALU.add))
    for _ in range(3):
        link(dve.tensor_tensor(t, y, y, ALU.mult))
        link(dve.tensor_tensor(t, t, half, ALU.mult))
        link(dve.scalar_tensor_tensor(y, t, 1.5, y, ALU.add, ALU.mult))


def layer_program(nc, A, out):
    f32, f32r = mybir.dt.float32, mybir.dt.float32r
    i32, u32 = mybir.dt.int32, mybir.dt.uint32
    ALU, ACT, AX = mybir.AluOpType, mybir.ActivationFunctionType, mybir.AxisListType

    root = ExitStack()
    with root:
        def sem(name):
            return root.enter_context(nc.semaphore(name))

        own_dve, own_pool, own_act = ([sem(n), 0] for n in ("own_dve", "own_pool", "own_act"))

        def tile_in(stack):
            def sb(name, shape, dt=f32):
                return stack.enter_context(nc.sbuf_tensor(name, shape, dt))
            return sb

        sb = tile_in(root)
        PS = root.enter_context(nc.psum_tensor("PS", [P, 8, 512], f32))

        def pair(n):
            return PS[:, 2 * n:2 * n + 2, :].rearrange("p a n -> p (a n)")

        ident = sb("ident", [P, P])

        xn2_d = nc.dram_tensor("xn2_d", (T, D), f32).ap()
        h_d = nc.dram_tensor("h_d", (T, D), f32).ap()
        token_d = nc.dram_tensor("token_d", (NE * T, 1), u32).ap()
        att_d = nc.dram_tensor("att_d", (P, CT, T), f32).ap()
        ys_d = nc.dram_tensor("ys_d", (NSLOT, D), f32).ap()
        pad_d = nc.dram_tensor("pad_d", (P, 2), u32).ap()
        item_d = nc.dram_tensor("item_d", (P, 5), i32).ap()

        small = ExitStack()
        mix = ExitStack()
        sb_small, sb_mix = tile_in(small), tile_in(mix)
        gates = sb("gates", [P, NT, TOPK])
        slots_u = sb("slots_u", [P, NT * TOPK], u32)

        ones = sb_small("ones", [P, P])
        later = sb_small("later", [P, P])
        rb_b = sb_small("rb_b", [P, NE])

        merge = sb_mix("merge", [P, len(LEVELS), P])
        causal2 = sb_mix("causal2", [P, 2, P])
        starts = sb_mix("starts", [P, 512])
        heads2 = sb_mix("heads2", [P, 2])
        mu_c = sb_mix("mu_c", [P, 14])
        omu_c = sb_mix("omu_c", [P, 14])
        par_c = sb_mix("par_c", [P, 5, CT])
        subg_b = sb_mix("subg_b", [P, P])
        hsel = sb_mix("hsel", [P, CT, NG])
        hspread = sb_mix("hspread", [NG, CT, P])
        lamt = sb_mix("lamt", [P, 8])

        rT = sb_mix("rT", [P, CT, T])
        kT = sb_mix("kT", [P, CT, T])
        vT = sb_mix("vT", [P, CT, T])
        loT = sb_mix("loT", [P, 2, T])

        att = ExitStack()
        sb_att = tile_in(att)
        qcT = sb_att("qcT", [P, CT, T])
        kcT = sb_att("kcT", [P, CT, T])
        vd = sb_att("vd", [P, NT, W])
        dist = sb_att("dist", [P, T])

        with ExitStack() as st:
            sbp = tile_in(st)
            wh = sbp("win_head", [P, 2, KT, P], f32r)
            wl = sbp("win_rest", [P, 2, KT, P], f32r)
            wf = sbp("win", [P, 2, KT, P])
            xh = sbp("x_head", [P, KT, T], f32r)
            xl = sbp("x_rest", [P, KT, T], f32r)
            xin = [t[:, j, :] for t in (qcT, kcT) for j in range(CT)]
            g1b = vd[:, 4:6, :].rearrange("p a n -> p (a n)")
            ssq = sbp("ssq", [P, NT])
            rstd = sbp("rstd", [P, 4, NT])
            scratch = vd.rearrange("p t n -> p (t n)")
            same = scratch[:, 0:(len(LEVELS) + 1) * P].rearrange("p (l n) -> p l n", n=P)
            lqk = scratch[:, 1024:1024 + 4 * HD].rearrange("p (l n) -> p l n", n=HD)
            s_msk, s_par, s_lam, s_mul, s_omu, s_id = (sem(n) for n in ("s_msk", "s_par", "s_lam", "s_mul", "s_omu", "s_id"))
            s_slot0 = sem("s_slot0")
            s_g1, s_wr = sem("s_g1"), (sem("s_w0"), sem("s_w1"))
            s_xi = [sem(f"s_xi{j}") for j in range(NT // 2)]
            s_wh, s_wl = sem("s_wh"), sem("s_wl")
            s_sq, s_xs, s_tr, s_trA, s_trD = sem("s_sq"), sem("s_xs"), sem("s_tr"), sem("s_trA"), sem("s_trD")
            s_pj, s_evA, s_evD = sem("s_pj"), sem("s_evA"), sem("s_evD")
            NC_ = 22
            NR = 14
            NW = NC_ + CT
            x_rows = A["x"][0].rearrange("(j p) d -> j p d", p=P)
            w_in = A["w_in"][0].rearrange("(k p) n -> p k n", p=P)

            with nc.Block() as block:
                def quarter(j, hf):
                    return (PS[:, 2 * (j % 2) + hf, :].rearrange("p (a n) -> p a n", a=4),
                            (slice(None), slice(4 * hf, 4 * hf + 4), slice(j * P, (j + 1) * P)))

                def target(n):
                    return (rT[:, n % 4, :], kT[:, n % 4, :], vT[:, n % 4, :], loT[:, n % 2, :])[n // 4]

                @block.gpsimd
                def _(pool):
                    link = linker(pool, own_pool)
                    link(pool.memset(starts[:, :], 0.0))
                    link(pool.memset(ident[:, :], 0.0))
                    link(pool.affine_select(out=ident[:, :], in_=ident[:, :], compare_op=ALU.not_equal, fill=1.0,
                                            base=0, pattern=[[-1, P]], channel_multiplier=1))
                    pool.sem_inc(s_id, 1)
                    link(pool.memset(ones[:, :], 1.0))
                    link(pool.memset(same[:, :, :], 1.0))
                    for n in range(len(LEVELS) + 1):
                        b = 1 << n
                        v = same[:, n, :].rearrange("p (j b) -> p j b", b=b)
                        link(pool.affine_select(out=v, in_=v, compare_op=ALU.is_ge, fill=0.0, base=0,
                                                pattern=[[-b, P // b], [0, b]], channel_multiplier=1))
                        link(pool.affine_select(out=v, in_=v, compare_op=ALU.is_ge, fill=0.0, base=b - 1,
                                                pattern=[[b, P // b], [0, b]], channel_multiplier=-1))
                    link(pool.affine_select(out=later[:, :], in_=ones[:, :], compare_op=ALU.is_gt, fill=0.0,
                                            base=0, pattern=[[1, P]], channel_multiplier=-1))
                    chunk = same[:, len(LEVELS), :]
                    for n, op in enumerate((ALU.is_gt, ALU.is_ge)):
                        link(pool.affine_select(out=causal2[:, n, :], in_=chunk, compare_op=op, fill=0.0,
                                                base=0, pattern=[[1, P]], channel_multiplier=-1))
                    for n in range(len(LEVELS)):
                        link(pool.tensor_tensor(merge[:, n, :], same[:, n + 1, :], same[:, n, :], ALU.subtract))
                    link(pool.memset(hsel[:, :, :], 0.0))
                    for c in range(CT):
                        link(pool.tensor_copy(hsel[:, c, 2 * c:2 * c + 2], chunk.rearrange("p (a n) -> p a n", n=HD)[:, :, 0]))
                    link(pool.memset(hspread[:, :, :], 1.0))
                    link(pool.affine_select(out=hspread[:, :, :], in_=hspread[:, :, :], compare_op=ALU.is_ge, fill=0.0,
                                            base=0, pattern=[[P, CT], [1, P]], channel_multiplier=-HD))
                    link(pool.affine_select(out=hspread[:, :, :], in_=hspread[:, :, :], compare_op=ALU.is_ge, fill=0.0,
                                            base=HD - 1, pattern=[[-P, CT], [-1, P]], channel_multiplier=HD))
                    link(pool.tensor_copy(heads2[:, :], chunk.rearrange("p (a n) -> p a n", n=HD)[:, :, 0]))
                    pool.sem_inc(s_msk, 1)
                    link(pool.iota(dist[:, :].bitcast(i32), [[1, T]], base=-(T - P), channel_multiplier=-1))
                    link(pool.tensor_copy(dist[:, :], dist[:, :].bitcast(i32)))
                    link(pool.affine_select(out=dist[:, :], in_=dist[:, :], compare_op=ALU.is_ge, fill=NEG,
                                            base=T - P, pattern=[[-1, T]], channel_multiplier=1))

                @block.sync
                def _(sp):
                    sp.dma_start(g1b[:, :], A["norm1_g"][0].partition_broadcast(P)).then_inc(s_g1, 16)
                    for j in range(NT):
                        sp.dma_start(xin[j], x_rows[j]).then_inc(s_xi[j // 2], 16)

                    def weights(n):
                        sp.dma_start(wf[:, n % 2, :, :], w_in[:, :, n * P:(n + 1) * P]).then_inc(s_wr[n % 2], 16)

                    weights(0)
                    weights(1)

                    def col(v, n):
                        return v.rearrange("(c p) -> p c", p=P, c=n)
                    with nc.allow_non_contiguous_dma(reason="small parameters by channel"):
                        sp.dma_start(mu_c[:, :], col(A["rwkv_mu"][0], 14)).then_inc(s_par, 16)
                        rk = A["rwkv_rk"][0].rearrange("h d -> (h d)")
                        for n, v in enumerate((A["rwkv_w0"][0], A["rwkv_a0"][0], A["rwkv_kk"][0], A["rwkv_ka"][0], rk)):
                            sp.dma_start(par_c[:, n, :], col(v, CT)).then_inc(s_par, 16)
                    sp.dma_start(subg_b[:, :], A["diff_subln_g"][0].partition_broadcast(P)).then_inc(s_par, 16)
                    for n, k in enumerate(("diff_lq1", "diff_lk1", "diff_lq2", "diff_lk2")):
                        sp.dma_start(lqk[:, n, :], A[k][0].partition_broadcast(P)).then_inc(s_par, 16)
                    sp.dma_start(rb_b[:, :], A["router_b"][0].partition_broadcast(P)).then_inc(s_par, 16)
                    sp.wait_ge(s_id, 1)
                    n0 = NE * T // P
                    sp.dma_start(token_d.rearrange("(p n) a -> p (n a)", p=P),
                                 starts[:, 0:n0].bitcast(u32)).then_inc(s_slot0, 16)
                    for n in range(2, NW):
                        sp.wait_ge(s_pj, n - 1 if n < NC_ + 2 else NC_ + 8)
                        weights(n)

                @block.scalar
                def _(act):
                    def head(n):
                        act.wait_ge(s_wr[n % 2], 16 * (n // 2 + 1))
                        act.activation(wh[:, n % 2, :, :], wf[:, n % 2, :, :], ACT.Copy).then_inc(s_wh, 1)

                    def square(j):
                        act.wait_ge(s_xi[j // 2], 32)
                        act.activation(pair(3), xin[j], ACT.Square, accum_out=ssq[:, j:j + 1]).then_inc(s_sq, 1)
                        act.wait_ge(s_sq, j + 1)

                    for j in range(4):
                        square(j)
                    for j in range(NT):
                        for hf in range(2):
                            act.wait_ge(s_tr, 2 * j + hf + 1)
                            src, dst = quarter(j, hf)
                            act.activation(xh[dst], src, ACT.Copy).then_inc(s_trA, 1)
                        if j + 4 < NT:
                            square(j + 4)
                        if j >= NT - 2:
                            head(j - NT + 2)
                    act.wait_ge(s_mul, 2)
                    act.activation(lamt[:, 2:4], lamt[:, 0:2], ACT.Exp).then_inc(s_lam, 1)
                    act.wait_ge(s_omu, 1)
                    for n in range(NC_):
                        act.wait_ge(s_pj, n + 1)
                        if n < NR:
                            dst = target(n)
                            act.activation(dst, pair(n % 4), ACT.Copy, scale=omu_c[:, n:n + 1]).then_inc(s_evA, 1)
                        elif n < NR + CT:
                            act.activation(qcT[:, n - NR, :], pair(n % 4), ACT.Copy,
                                           scale=float(HD) ** -0.5).then_inc(s_evA, 1)
                        else:
                            act.activation(kcT[:, n - NR - CT, :], pair(n % 4), ACT.Copy).then_inc(s_evA, 1)
                        head(n + 2)
                    act.wait_ge(s_msk, 1)
                    for n in range(2 * NT):
                        act.wait_ge(s_pj, NC_ + n + 1)
                        act.activation(vd[:, n % NT, n // NT * 256:(n // NT + 1) * 256], PS[:, n % 8, 0:256],
                                       ACT.Copy).then_inc(s_evA, 1)
                        if n == NT - 1:
                            head(NW - 2)
                            head(NW - 1)

                @block.vector
                def _(dve):
                    link = linker(dve, own_dve)
                    dve.wait_ge(s_g1, 16)

                    def rest(n):
                        dve.wait_ge(s_wh, n + 1)
                        dve.tensor_tensor(wl[:, n % 2, :, :], wf[:, n % 2, :, :], wh[:, n % 2, :, :].bitcast(f32),
                                          ALU.subtract).then_inc(s_wl, 1)

                    def scale(j):
                        if j % 2 == 0:
                            dve.wait_ge(s_sq, j + 2)
                            r = [rstd[:, n, j:j + 2] for n in range(4)]
                            link(dve.tensor_scalar(r[1], ssq[:, j:j + 2], 1.0 / D, NORM_EPS, ALU.mult, ALU.add))
                            inverse_root(dve, link, *r)
                        dve.scalar_tensor_tensor(xin[j], xin[j], rstd[:, 0, j:j + 1], g1b, ALU.mult, ALU.mult).then_inc(s_xs, 1)

                    scale(0)
                    scale(1)
                    for j in range(NT):
                        if j + 2 < NT:
                            scale(j + 2)
                        for hf in range(2):
                            dve.wait_ge(s_trA, 2 * j + hf + 1)
                            src, dst = quarter(j, hf)
                            dve.tensor_tensor(xl[dst], src, xh[dst].bitcast(f32), ALU.subtract).then_inc(s_trD, 1)
                        if j >= NT - 2:
                            rest(j - NT + 2)
                    dve.wait_ge(s_par, 16 * 12)
                    link(dve.tensor_scalar(omu_c[:, :], mu_c[:, :], -1.0, 1.0, ALU.mult, ALU.add))
                    dve.sem_inc(s_omu, 1)
                    link(dve.tensor_scalar(subg_b[:, :], subg_b[:, :], 1.0 - LAMBDA_INIT, None, ALU.mult))
                    for n in range(2):
                        dve.tensor_tensor_reduce(out=lqk[:, 2 * n, :], in0=lqk[:, 2 * n, :], in1=lqk[:, 2 * n + 1, :],
                                                 scale=1.0, scalar=0.0, op0=ALU.mult, op1=ALU.add,
                                                 accum_out=lamt[:, n:n + 1]).then_inc(s_mul, 1)
                    dve.wait_ge(s_lam, 1)
                    link(dve.tensor_tensor(lamt[:, 4:5], lamt[:, 3:4], lamt[:, 2:3], ALU.subtract))
                    link(dve.tensor_scalar(lamt[:, 5:6], lamt[:, 4:5], -LAMBDA_INIT, None, ALU.add))
                    dve.wait_ge(s_slot0, 16)
                    link(dve.memset(starts[:, :], 1.0))
                    link(dve.memset(starts[:, :].rearrange("p (a n) -> p a n", n=HD)[:, :, 0], 0.0))
                    for n in range(NR):
                        dve.wait_ge(s_evA, n + 1)
                        dst = target(n)
                        dve.scalar_tensor_tensor(dst[:, 1:T], pair(n % 4)[:, 0:T - 1], mu_c[:, n:n + 1], dst[:, 1:T],
                                                 ALU.mult, ALU.add).then_inc(s_evD, 1)
                        rest(n + 2)
                    for n in range(NR + 2, NW):
                        rest(n)

                @block.tensor
                def _(pe):
                    pe.wait_ge(s_id, 1)
                    for j in range(NT):
                        pe.wait_ge(s_xs, j + 1)
                        for k in range(KT):
                            if j >= 2 and k % 4 == 0:
                                pe.wait_ge(s_trD, 2 * (j - 2) + k // 4 + 1)
                            ins = pe.transpose(PS[:, 2 * (j % 2) + k // 4, (k % 4) * P:(k % 4 + 1) * P],
                                               xin[j][:, k * P:(k + 1) * P], ident[:, :])
                            if k % 4 == 3:
                                ins.then_inc(s_tr, 1)
                    pe.wait_ge(s_trD, 2 * NT)
                    parts = ((0, 0), (0, 1), (1, 0))
                    for n in range(NC_):
                        pe.wait_ge(s_wl, n + 1)
                        if n >= 4:
                            pe.wait_ge(s_evA, n - 3)
                            pe.wait_ge(s_evD, min(n - 3, NR))
                        for th in range(2):
                            for k in range(KT):
                                for a, b in parts:
                                    ins = pe.matmul(PS[:, 2 * (n % 4) + th, :], (wh, wl)[a][:, n % 2, k, :],
                                                    (xh, xl)[b][:, k, th * 512:(th + 1) * 512],
                                                    start=(k == 0 and a == b), stop=(k == KT - 1 and a == 1))
                        ins.then_inc(s_pj, 1)
                    for n in range(2 * NT):
                        pe.wait_ge(s_wl, NC_ + 2 * (n // NT) + 2)
                        pe.wait_ge(s_evA, NC_ + max(0, n - 7))
                        j = n % NT
                        for k in range(KT):
                            for a, b in parts:
                                ins = pe.matmul(PS[:, n % 8, 0:256], (xh, xl)[b][:, k, j * P:(j + 1) * P],
                                                (wh, wl)[a][:, :, k, :],
                                                start=(k == 0 and a == b), stop=(k == KT - 1 and a == 1))
                        ins.then_inc(s_pj, 1)

        UN = NT * CT
        with ExitStack() as st:
            sba = tile_in(st)
            alibi = sba("alibi", [P, CT, T])
            scs = [sba(f"sc{n}", [P, 2, T]) for n in range(3)]
            aT = sba("aT", [P, 2, NT, P])
            osb = sba("osb", [P, 2, CT, P])
            st8 = sba("st8", [P, 2, 6])
            fac = sba("fac", [P, 4, 2])
            no2 = sba("no2", [P, 5, CT])
            osq = sba("osq", [P, P])
            attT = sba("attT", [P, CT, T])
            a_al = sem("a_al")
            a_s, a_mx, a_ex, a_cb, a_t, a_te = (sem(n) for n in ("a_s", "a_mx", "a_ex", "a_cb", "a_t", "a_te"))
            a_o, a_oe, a_sq, a_n, a_f, a_fe = (sem(n) for n in ("a_o", "a_oe", "a_sq", "a_n", "a_f", "a_fe"))
            a_nm, a_out, a_nr = sem("a_nm"), sem("a_out"), sem("a_nr")
            with nc.Block() as block:
                @block.sync
                def _(sp):
                    for i in range(NT):
                        sp.wait_ge(a_fe, i + 1)
                        sp.dma_start(att_d[:, :, i * P:(i + 1) * P], attT[:, :, i * P:(i + 1) * P]).then_inc(a_out, 16)
                    sp.wait_ge(a_out, 16 * NT)

                def width(n):
                    return (n // CT + 1) * P

                @block.tensor
                def _(pe):
                    def scores(n):
                        i, h = n // CT, n % CT
                        if n >= 1:
                            pe.wait_ge(a_mx, 2 * n)
                        for m in range(2):
                            for c0 in range(0, width(n), 512):
                                w = min(512, width(n) - c0)
                                ins = pe.matmul(PS[:, 2 * m + c0 // 512, 0:w], qcT[64 * m:64 * m + 64, h, i * P:(i + 1) * P],
                                                kcT[64 * m:64 * m + 64, h, c0:c0 + w], start=True, stop=True)
                        ins.then_inc(a_s, 1)

                    def turn(n):
                        i = n // CT
                        pe.wait_ge(a_cb, n + 1)
                        if n >= 1:
                            pe.wait_ge(a_te, n)
                        for k in range(i + 1):
                            ins = pe.transpose(PS[:, 4 + k // 4, (k % 4) * P:(k % 4 + 1) * P],
                                               scs[n % 3][:, 0, k * P:(k + 1) * P], ident[:, :])
                        ins.then_inc(a_t, 1)

                    def values(n):
                        i, h = n // CT, n % CT
                        pe.wait_ge(a_te, n + 1)
                        if n >= 1:
                            pe.wait_ge(a_oe, n)
                        for k in range(i + 1):
                            ins = pe.matmul(PS[:, 6, 0:P], aT[:, n % 2, k, :], vd[:, k, h * P:(h + 1) * P],
                                            start=(k == 0), stop=(k == i))
                        ins.then_inc(a_o, 1)

                    def flip(i):
                        pe.wait_ge(a_n, CT * (i + 1))
                        if i >= 1:
                            pe.wait_ge(a_fe, i)
                        for h in range(CT):
                            ins = pe.transpose(PS[:, 7, h * P:(h + 1) * P], osb[:, i % 2, h, :], ident[:, :])
                        ins.then_inc(a_f, 1)

                    scores(0)
                    for n in range(UN):
                        if n + 1 < UN:
                            scores(n + 1)
                        if n >= 1:
                            turn(n - 1)
                        if n >= 2:
                            values(n - 2)
                        if n >= CT and n % CT == 3:
                            flip(n // CT - 1)
                    turn(UN - 1)
                    values(UN - 2)
                    values(UN - 1)
                    flip(NT - 1)

                @block.vector
                def _(dve):
                    link = linker(dve, own_dve)
                    def maxima(n):
                        i, h = n // CT, n % CT
                        dve.wait_ge(a_s, n + 1)
                        dve.wait_ge(a_al, h + 1)
                        if n >= 3:
                            dve.wait_ge(a_t, n - 2)
                        w = width(n)
                        for m in range(2):
                            dve.tensor_tensor_reduce(out=scs[n % 3][:, m, 0:w], in0=pair(m)[:, 0:w],
                                                     in1=alibi[:, h, T - w:T], scale=1.0, scalar=NEG, op0=ALU.add, op1=ALU.max,
                                                     accum_out=st8[:, n % 2, m:m + 1]).then_inc(a_mx, 1)
                        dve.wait_ge(a_mx, 2 * n + 2)
                        dve.tensor_scalar(st8[:, n % 2, 2:4], st8[:, n % 2, 0:2], -1.0, None, ALU.mult).then_inc(a_nm, 1)

                    def combine(n):
                        w = width(n)
                        dve.wait_ge(a_ex, 2 * n + 2)
                        sums, f = st8[:, n % 2, 4:6], fac[:, n % 4, :]
                        link(dve.reciprocal(f[:, 0:2], sums))
                        link(dve.scalar_tensor_tensor(f[:, 1:2], f[:, 1:2], lamt[:, 5:6], sums[:, 0:1], ALU.mult, ALU.mult))
                        dve.scalar_tensor_tensor(scs[n % 3][:, 0, 0:w], scs[n % 3][:, 1, 0:w], f[:, 1:2],
                                                 scs[n % 3][:, 0, 0:w], ALU.mult, ALU.add).then_inc(a_cb, 1)

                    def norm(i):
                        dve.wait_ge(a_sq, CT * (i + 1))
                        t = [no2[:, n, :] for n in range(5)]
                        dve.tensor_scalar(t[2], t[0], 1.0 / P, NORM_EPS, ALU.mult, ALU.add).then_inc(a_nr, 1)
                        dve.wait_ge(a_nr, i + 1)
                        inverse_root(dve, link, *t[1:])
                        for h in range(CT):
                            dve.scalar_tensor_tensor(osb[:, i % 2, h, :], osb[:, i % 2, h, :], t[1][:, h:h + 1], subg_b[:, :],
                                                     ALU.mult, ALU.mult).then_inc(a_n, 1)

                    maxima(0)
                    for n in range(UN):
                        if n + 1 < UN:
                            maxima(n + 1)
                        combine(n)
                        if n >= CT and n % CT == 2:
                            norm(n // CT - 1)
                    norm(NT - 1)

                @block.scalar
                def _(act):
                    def exps(n):
                        act.wait_ge(a_nm, n + 1)
                        for m in range(2):
                            v = scs[n % 3][:, m, 0:width(n)]
                            act.activation(v, v, ACT.Exp, bias=st8[:, n % 2, 2 + m:3 + m],
                                           accum_out=st8[:, n % 2, 4 + m:5 + m]).then_inc(a_ex, 1)

                    def keys(n):
                        i = n // CT
                        act.wait_ge(a_t, n + 1)
                        if n >= 2:
                            act.wait_ge(a_o, n - 1)
                        flat = aT[:, n % 2, 0:i + 1, :].rearrange("p a n -> p (a n)")
                        act.activation(flat, pair(2)[:, 0:width(n)], ACT.Copy).then_inc(a_te, 1)

                    def rows(n):
                        i, h = n // CT, n % CT
                        act.wait_ge(a_o, n + 1)
                        if i >= 2:
                            act.wait_ge(a_f, i - 1)
                        act.activation(osb[:, i % 2, h, :], PS[:, 6, 0:P], ACT.Copy, scale=fac[:, n % 4, 0:1]).then_inc(a_oe, 1)
                        act.wait_ge(a_oe, n + 1)
                        if i >= 1:
                            act.wait_ge(a_nr, i)
                        act.activation(osq[:, :], osb[:, i % 2, h, :], ACT.Square,
                                       accum_out=no2[:, 0, h:h + 1]).then_inc(a_sq, 1)
                        act.wait_ge(a_sq, n + 1)

                    def done(i):
                        act.wait_ge(a_f, i + 1)
                        act.activation(attT[:, :, i * P:(i + 1) * P], PS[:, 7, :].rearrange("p (c n) -> p c n", c=CT),
                                       ACT.Copy).then_inc(a_fe, 1)

                    for h in range(CT):
                        act.activation(alibi[:, h, :], dist[:, :], ACT.Copy, scale=2.0 ** (-8.0 * (h + 1) / CT)).then_inc(a_al, 1)
                    exps(0)
                    for n in range(UN):
                        if n + 1 < UN:
                            exps(n + 1)
                        if n >= 1:
                            keys(n - 1)
                        if n >= 2:
                            rows(n - 2)
                        if n >= 2 * CT and n % CT == 0:
                            done(n // CT - 2)
                    keys(UN - 1)
                    rows(UN - 2)
                    done(NT - 2)
                    rows(UN - 1)
                    done(NT - 1)
        att.close()

        def head_of(g):
            return 2 * (g % CT) + g // CT

        with ExitStack() as st:
            sbr = tile_in(st)
            sgz, sga = sbr("sgz", [P, CT, T]), sbr("sga", [P, CT, T])
            lng_b, lnb_b = sbr("lng_b", [P, W]), sbr("lnb_b", [P, W])
            wab = sbr("wab", [P, W])
            gb = sbr("gb", [P, W])
            r_ln, r_lo = sem("r_ln"), sem("r_lo")
            cum, eL, eU, eN = (sbr(n, [P, CT, P]) for n in ("cum", "eL", "eU", "eN"))
            ld = eL
            kk, kn, be, ka = (sbr(n, [P, CT, P]) for n in ("kk", "kn", "be", "ka"))
            ar = sbr("ar", [P, 2, CT, 2, P])
            rkp = sbr("rkp", [P, 2, CT, P])
            pc = sbr("pc", [P, 2, CT, 2])
            tok = sbr("tok", [P, 2, 2, W])
            BG = sbr("BG", [P, 2, NG, 2, P])
            KG = sbr("KG", [P, 2, NG, 2, P])
            LM = sbr("LM", [P, 2, NG, P])
            XT = sbr("XT", [P, 2, NG, P])
            X = sbr("X", [P, NG, P])
            PM = sbr("PM", [P, NG, P])
            S = sbr("S", [P, CT, P])
            Rb, Un = loT[:, 0, 0:W], loT[:, 0, W:2 * W]
            ysb = sbr("ysb", [P, W])
            gn = sbr("gn", [P, 4, NG])
            Sq = wab[:, :].rearrange("p (h n) -> p h n", n=HD)
            rn = sbr("rn", [NG, T])
            gr = sbr("gr", [P, 3, NG])
            r_s8, r_n8, r_rt, r_ri = sem("r_s8"), sem("r_n8"), sem("r_rt"), sem("r_ri")
            NL = len(LEVELS)
            r_act, r_z, r_ze = sem("r_act"), sem("r_z"), sem("r_ze")
            r_cum, r_exp, r_kr, r_ss, r_rn = (sem(n) for n in ("r_cum", "r_exp", "r_kr", "r_ss", "r_rn"))
            r_kp, r_pD, r_pP, r_tr, r_te, r_g, r_ge = (sem(n) for n in ("r_kp", "r_pD", "r_pP", "r_tr", "r_te", "r_g", "r_ge"))
            r_lm, r_x0, r_P, r_Pe, r_X, r_Xe, r_T, r_Te = (sem(n) for n in ("r_lm", "r_x0", "r_P", "r_Pe", "r_X", "r_Xe", "r_T", "r_Te"))
            q_0, q_R, q_Re, q_U, q_Ue, q_S, q_Se, q_Y = (sem(n) for n in ("q_0", "q_R", "q_Re", "q_U", "q_Ue", "q_S", "q_Se", "q_Y"))
            q_y1, q_bg, q_y2, q_f, q_yT, q_pcw = (sem(n) for n in ("q_y1", "q_bg", "q_y2", "q_f", "q_yT", "q_pcw"))

            def cut(a, i):
                return a[:, :, i * P:(i + 1) * P]

            def by_c(n):
                return par_c[:, n, :].unsqueeze(2).to_broadcast([P, CT, P])

            def over_heads(m, n):
                return m.unsqueeze(1).to_broadcast([P, n, P])

            with nc.Block() as block:
                @block.sync
                def _(sp):
                    sp.dma_start(wab[0:64, :], A["rwkv_wb"][0]).then_inc(r_lo, 16)
                    sp.dma_start(wab[64:128, :], A["rwkv_ab"][0]).then_inc(r_lo, 16)
                    sp.dma_start(gb[:, :], A["rwkv_gb"][0]).then_inc(r_lo, 16)
                    sp.dma_start(lng_b[:, :], A["rwkv_ln_g"][0].partition_broadcast(P)).then_inc(r_ln, 16)
                    sp.dma_start(lnb_b[:, :], A["rwkv_ln_b"][0].partition_broadcast(P)).then_inc(r_ln, 16)

                @block.tensor
                def _(pe):
                    pe.wait_ge(r_act, 1)
                    pe.wait_ge(r_lo, 48)
                    for n in range(2 * CT):
                        c, th = n // 2, n % 2
                        if n >= 4:
                            pe.wait_ge(r_ze, 2 * (n - 3))
                        for a in range(2):
                            pe.matmul(PS[:, 4 * a + n % 4, :], wab[64 * a:64 * a + 64, c * P:(c + 1) * P],
                                      loT[64 * a:64 * a + 64, 0, th * 512:(th + 1) * 512],
                                      start=True, stop=True).then_inc(r_z, 1)
                    pe.wait_ge(r_ze, 4 * CT)

                    for n in range(2 * CT):
                        th, c = n // CT, n % CT
                        pe.wait_ge(r_s8, n + 1)
                        pe.matmul(PS[0:NG, th, :], hsel[:, c, :], (kn, be)[n % 2][:, :, :].rearrange("p c n -> p (c n)"),
                                  start=(c == 0), stop=(c == CT - 1)).then_inc(r_n8, 1)
                    pe.wait_ge(r_ri, 1)

                    def norms(i):
                        if i >= 2:
                            pe.wait_ge(r_ri, 2)
                        if i >= 3:
                            pe.wait_ge(q_y2, i - 2)
                        for c in range(CT):
                            ins = pe.matmul(PS[:, 6, c * P:(c + 1) * P], hspread[:, c, :], rn[:, i * P:(i + 1) * P],
                                            start=True, stop=True)
                        ins.then_inc(r_ss, 1)

                    def grams(i):
                        pe.wait_ge(r_pD, i + 1)
                        pe.wait_ge(r_pP, i + 1)
                        if i >= 1:
                            pe.wait_ge(r_Te, 2 * (NL) * i)
                            pe.wait_ge(r_Xe, 2 * (NL - 1) * i)
                        for n, src in enumerate((be, ka, None)):
                            for c in range(CT):
                                v = src[:, c, :] if src is not None else vT[:, c, i * P:(i + 1) * P]
                                ins = pe.transpose(PS[:, 1 + n, c * P:(c + 1) * P], v, ident[:, :])
                            ins.then_inc(r_tr, 1)
                        for n, src in enumerate((be, ka)):
                            for g in range(NG):
                                b, hp, c = g // 2, g // CT, g % CT
                                if g % 2 == 0:
                                    if n == 0 and b > 0:
                                        pe.wait_ge(r_te, 3 * i + b)
                                    if n == 1:
                                        pe.wait_ge(r_ge, 8 * i + b + 1)
                                ins = pe.matmul(PS[:, b, (g % 2) * 256:(g % 2) * 256 + 256],
                                                src[64 * hp:64 * hp + 64, c, :],
                                                ar[64 * hp:64 * hp + 64, i % 2, c, :, :].rearrange("p a n -> p (a n)"),
                                                start=True, stop=True)
                                if g % 2 == 1:
                                    ins.then_inc(r_g, 1)

                    def flip(i, l, src):
                        for hf in range(2):
                            if l == 0:
                                pe.wait_ge(r_x0, i + 1)
                                pe.wait_ge(r_ge, 8 * i + 8)
                            else:
                                pe.wait_ge(r_Xe, 2 * (NL - 1) * i + 2 * (l - 1) + hf + 1)
                                pe.wait_ge(r_Pe, 2 * (NL - 1) * i + 2 * (l - 1) + hf + 1)
                            for g in range(4 * hf, 4 * hf + 4):
                                ins = pe.transpose(PS[:, hf, (g % 4) * P:(g % 4 + 1) * P], src[:, g, :], ident[:, :])
                            ins.then_inc(r_T, 1)

                    def level_P(i, l):
                        pe.wait_ge(r_lm, NL * i + l + 1)
                        for hf in range(2):
                            pe.wait_ge(r_Te, 2 * NL * i + 2 * l - 1 + hf)
                            for g in range(4 * hf, 4 * hf + 4):
                                ins = pe.matmul(PS[:, hf, (g % 4) * P:(g % 4 + 1) * P], LM[:, l % 2, g, :], X[:, g, :],
                                                start=True, stop=True)
                            ins.then_inc(r_P, 1)

                    def level_X(i, l):
                        for hf in range(2):
                            pe.wait_ge(r_Pe, 2 * (NL - 1) * i + 2 * (l - 1) + hf + 1)
                            if l >= 2:
                                pe.wait_ge(r_Xe, 2 * (NL - 1) * i + 2 * (l - 2) + hf + 1)
                            for g in range(4 * hf, 4 * hf + 4):
                                ins = pe.matmul(PS[:, 2 + hf, (g % 4) * P:(g % 4 + 1) * P], XT[:, i % 2, g, :],
                                                PM[:, g, :], start=True, stop=True)
                            ins.then_inc(r_X, 1)

                    def state_term(i, cp, half, bank, **kw):
                        for c in range(CT):
                            ins = pe.matmul(PS[64 * cp:64 * cp + 64, bank, c * P:(c + 1) * P],
                                            ar[:, i % 2, c, half, 64 * cp:64 * cp + 64], S[:, c, :],
                                            start=False, stop=True, skip_group_check=True)
                        return ins

                    def head_term(i, bank, lhs, rhs, first):
                        for g in range(NG):
                            h = head_of(g)
                            ins = pe.matmul(PS[:, bank, h * HD:(h + 1) * HD], lhs(g),
                                            rhs[:, h // 2, (h % 2) * HD:(h % 2 + 1) * HD],
                                            start=(first and g == 0), stop=True, skip_group_check=True)
                        return ins

                    def seq(i, s):
                        q = i % 2
                        v = cut(vT, i)
                        if s == 0:
                            pe.wait_ge(q_0, 1)
                            pe.wait_ge(r_ge, 8 * i + 8)
                            pe.wait_ge(r_te, 3 * i + 3)
                            if i >= 1:
                                pe.wait_ge(q_yT, i)
                                pe.wait_ge(q_Se, 4 * i)
                            head_term(i, 4, lambda g: KG[:, q, g, 0, :], v, True)
                            state_term(i, 0, 0, 4).then_inc(q_R, 1)
                        if s in (1, 4):
                            cp = s // 4
                            pe.wait_ge(q_Re, 2 * i + cp + 1)
                            pe.wait_ge(r_Te, 2 * NL * (i + 1))
                            if i >= 1:
                                pe.wait_ge(q_y2, i)
                            for g in range(NG):
                                h = head_of(g)
                                ins = pe.matmul(PS[64 * cp:64 * cp + 64, 5, h * HD:(h + 1) * HD],
                                                XT[:, q, g, 64 * cp:64 * cp + 64], Rb[:, h * HD:(h + 1) * HD],
                                                start=True, stop=True)
                            ins.then_inc(q_U, 1)
                            if s == 1:
                                if i >= 1:
                                    pe.wait_ge(q_y1, i)
                                head_term(i, 7, lambda g: KG[:, q, g, 1, :], v, True)
                            state_term(i, cp, 1, 7)
                        if s in (2, 5):
                            cp = s // 5
                            rows = slice(64 * cp, 64 * cp + 64)
                            pe.wait_ge(q_Ue, 2 * i + cp + 1)
                            if i + 2 < NT:
                                pe.wait_ge(r_rn, i + 3)
                            if cp:
                                pe.wait_ge(q_Se, 4 * i + 2)
                            for c in range(CT):
                                cols = slice(c * P, (c + 1) * P)
                                pe.matmul(PS[:, 6, cols], tok[rows, q, 1, cols], v[rows, c, :],
                                          start=(c == 0), stop=False, skip_group_check=True)
                            for c in range(CT):
                                cols = slice(c * P, (c + 1) * P)
                                ins = pe.matmul(PS[:, 6, cols], tok[rows, q, 0, cols], Un[rows, cols],
                                                start=False, stop=True, skip_group_check=True)
                            ins.then_inc(q_S, 1)
                            if cp:
                                head_term(i, 7, lambda g: BG[:, q, g, 1, :],
                                          Un[:, :].rearrange("p (c n) -> p c n", c=CT), False).then_inc(q_Y, 1)
                        if s == 3:
                            pe.wait_ge(q_Se, 4 * i + 2)
                            pe.wait_ge(q_Re, 2 * i + 1)
                            state_term(i, 1, 0, 4).then_inc(q_R, 1)
                        if s == 6:
                            pe.wait_ge(q_Se, 4 * i + 4)
                            pe.wait_ge(q_Ue, 2 * i + 2)
                            for c in range(CT):
                                pe.matmul(PS[:, 6, 2 * c:2 * c + 2], rkp[:, q, c, :], heads2[:, :], start=True, stop=True)
                            pe.matmul(PS[:, 5, :], loT[:, 1, i * P:(i + 1) * P], gb[:, :],
                                      start=True, stop=True).then_inc(q_bg, 1)
                        if s == 7:
                            pe.wait_ge(q_y2, i + 1)
                            pe.wait_ge(q_Re, 2 * i + 2)
                            for c in range(CT):
                                ins = pe.transpose(PS[:, 4, c * P:(c + 1) * P], ysb[:, c * P:(c + 1) * P], ident[:, :])
                            ins.then_inc(q_f, 1)

                    norms(0)
                    for i in range(NT):
                        grams(i)
                        flip(i, 0, XT[:, i % 2])
                        if i >= 2:
                            seq(i - 2, 7)
                        for l in range(1, NL):
                            level_P(i, l)
                            if l == 1 and i + 1 < NT:
                                norms(i + 1)
                            if i >= 1 and l <= 3:
                                seq(i - 1, 2 * l - 2)
                            if i >= 1 and l == 4:
                                seq(i - 1, 6)
                            level_X(i, l)
                            if i >= 1 and l <= 3:
                                seq(i - 1, 2 * l - 1)
                            flip(i, l, X)
                    seq(NT - 2, 7)
                    for s in range(8):
                        seq(NT - 1, s)

                @block.scalar
                def _(act):
                    link = linker(act, own_act)
                    act.activation(loT[0:64, 0, :], loT[0:64, 0, :], ACT.Tanh).then_inc(r_act, 1)
                    link(act.activation(loT[:, 1, :], loT[:, 1, :], ACT.Sigmoid))
                    for n in range(2 * CT):
                        c, th = n // 2, n % 2
                        for a in range(2):
                            act.wait_ge(r_z, 2 * n + a + 1)
                            act.activation((sgz, sga)[a][:, c, th * 512:(th + 1) * 512], PS[:, 4 * a + n % 4, :],
                                           ACT.Sigmoid, bias=par_c[:, a, c:c + 1]).then_inc(r_ze, 1)

                    for n in range(2 * CT):
                        th, c = n // CT, n % CT
                        if n >= 2:
                            act.wait_ge(r_n8, n - 1)
                        act.activation((kn, be)[n % 2][:, :, :].rearrange("p c n -> p (c n)"),
                                       kT[:, c, th * 512:(th + 1) * 512], ACT.Square,
                                       scale=par_c[:, 2, c:c + 1]).then_inc(r_s8, 1)
                    act.wait_ge(r_n8, 2 * CT)
                    act.activation(rn[:, :], pair(0)[0:NG, :], ACT.Sqrt).then_inc(r_rt, 1)

                    def exps(i):
                        act.wait_ge(r_cum, i + 1)
                        if i >= 1:
                            act.wait_ge(r_pD, i)
                            act.wait_ge(r_pP, i)
                        act.activation(eU[:, :, :], cum[:, :, :], ACT.Exp).then_inc(r_exp, 1)
                        act.activation(eN[:, :, :], cum[:, :, :], ACT.Exp, scale=-1.0).then_inc(r_exp, 1)
                        act.activation(eL[:, :, :], eL[:, :, :], ACT.Exp).then_inc(r_exp, 1)

                    def seq(i, s):
                        q = i % 2
                        if s in (1, 4):
                            cp = s // 4
                            rows = slice(64 * cp, 64 * cp + 64)
                            act.wait_ge(q_U, 2 * i + cp + 1)
                            if i >= 1:
                                act.wait_ge(q_Y, i)
                            act.activation(Un[rows, :], PS[rows, 5, :], ACT.Copy, scale=-1.0).then_inc(q_Ue, 1)
                        if s == 5:
                            act.wait_ge(q_Y, i + 1)
                            if i >= 1:
                                act.wait_ge(q_f, i)
                            act.activation(ysb[:, :], PS[:, 7, :], ACT.Copy).then_inc(q_y1, 1)
                        if s == 7:
                            act.wait_ge(q_f, i + 1)
                            act.activation(cut(rT, i), PS[:, 4, :].rearrange("p (c n) -> p c n", c=CT),
                                           ACT.Copy).then_inc(q_yT, 1)

                    exps(0)
                    for i in range(NT):
                        q = i % 2
                        for n in range(3):
                            act.wait_ge(r_tr, 3 * i + n + 1)
                            if i >= 2:
                                act.wait_ge(q_S, 2 * (i - 1))
                            dst = tok[:, q, n, :].rearrange("p (c n) -> p c n", c=CT) if n < 2 else cut(vT, i)
                            act.activation(dst, PS[:, 1 + n, :].rearrange("p (c n) -> p c n", c=CT),
                                           ACT.Copy).then_inc(r_te, 1)
                        for hf in range(2):
                            act.wait_ge(r_T, 2 * NL * i + hf + 1)
                            act.activation(X[:, 4 * hf:4 * hf + 4, :], PS[:, hf, :].rearrange("p (c n) -> p c n", c=4),
                                           ACT.Copy).then_inc(r_Te, 1)
                        if i >= 2:
                            seq(i - 2, 7)
                        for l in range(1, NL):
                            for hf in range(2):
                                act.wait_ge(r_P, 2 * (NL - 1) * i + 2 * (l - 1) + hf + 1)
                                act.activation(PM[:, 4 * hf:4 * hf + 4, :],
                                               PS[:, hf, :].rearrange("p (c n) -> p c n", c=4), ACT.Copy).then_inc(r_Pe, 1)
                            if l == 1 and i + 1 < NT:
                                exps(i + 1)
                            if i >= 1 and l <= 3:
                                seq(i - 1, 2 * l - 2)
                                seq(i - 1, 2 * l - 1)
                            for hf in range(2):
                                act.wait_ge(r_T, 2 * NL * i + 2 * l + hf + 1)
                                act.activation(XT[:, q, 4 * hf:4 * hf + 4, :],
                                               PS[:, hf, :].rearrange("p (c n) -> p c n", c=4), ACT.Copy).then_inc(r_Te, 1)
                    seq(NT - 2, 7)
                    for s in range(8):
                        seq(NT - 1, s)

                @block.gpsimd
                def _(pool):
                    link = linker(pool, own_pool)
                    link(pool.memset(S[:, :, :], 0.0))
                    pool.wait_ge(r_ze, 4 * CT)
                    link(pool.memset(Rb[:, :], 0.0))
                    pool.sem_inc(q_0, 1)

                    def raw(i):
                        if i >= 1:
                            pool.wait_ge(r_pD, i)
                        else:
                            pool.wait_ge(r_ri, 1)
                        pool.tensor_tensor(kk[:, :, :], cut(kT, i), by_c(2), ALU.mult).then_inc(r_kr, 1)

                    def rho(i):
                        pool.wait_ge(r_exp, 3 * i + 1)
                        if i >= 2:
                            pool.wait_ge(q_S, 2 * (i - 1))
                            pool.wait_ge(q_Se, 4 * (i - 1))
                            pool.wait_ge(q_bg, i - 1)
                        pool.tensor_tensor(ar[:, i % 2, :, 1, :], cut(rT, i), eU[:, :, :], ALU.mult).then_inc(q_pcw, 1)
                        link(pool.tensor_copy(pc[:, i % 2, :, :], eU[:, :, :].rearrange("p c (a n) -> p c a n", n=HD)[:, :, :, HD - 1]))
                        pool.wait_ge(r_kp, i + 1)
                        link(pool.tensor_tensor(rkp[:, i % 2, :, :], cut(rT, i), by_c(4), ALU.mult))
                        pool.wait_ge(q_pcw, i + 1)
                        pool.tensor_tensor(rkp[:, i % 2, :, :], rkp[:, i % 2, :, :], kn[:, :, :], ALU.mult).then_inc(r_pP, 1)

                    def part(i, l):
                        if l == 0:
                            pool.wait_ge(r_ge, 8 * i + 4)
                        if l == 2:
                            pool.wait_ge(r_x0, i + 1)
                        if l != 2 and (i or l > 2):
                            pool.wait_ge(r_P, 2 * (NL - 1) * i + 2 * (l - 2) if l > 2 else 2 * (NL - 1) * i - 2 * (1 - l))
                        pool.tensor_tensor(LM[:, l % 2, :, :], BG[:, i % 2, :, 0, :], over_heads(merge[:, l, :], NG),
                                           ALU.mult).then_inc(r_lm, 1)

                    raw(0)
                    rho(0)
                    for i in range(NT):
                        if i + 1 < NT:
                            raw(i + 1)
                        for l in range(NL):
                            part(i, l)
                            if l == NL - 1 and i + 1 < NT:
                                rho(i + 1)

                @block.vector
                def _(dve):
                    link = linker(dve, own_dve)
                    dve.wait_ge(r_ze, 4 * CT)
                    dve.wait_ge(r_rt, 1)
                    dve.wait_ge(r_ln, 32)
                    link(dve.tensor_scalar(rn[:, :], rn[:, :], 1e-12, None, ALU.max))
                    dve.reciprocal(rn[:, 0:2 * P], rn[:, 0:2 * P]).then_inc(r_ri, 1)

                    def decay(i):
                        if i >= 1:
                            dve.wait_ge(r_exp, 3 * i)
                            dve.wait_ge(r_pD, i)
                        link(dve.tensor_scalar(ld[:, :, :], cut(sgz, i), -0.6065306597126334, None, ALU.mult))
                        flat = [t[:, :, :].rearrange("p c n -> p (c n)") for t in (cum, ld)]
                        link(dve.tensor_tensor_scan(flat[0], starts[:, :], flat[1], 0.0, ALU.mult, ALU.add))
                        dve.tensor_tensor(eL[:, :, :], cum[:, :, :], ld[:, :, :], ALU.subtract).then_inc(r_cum, 1)

                    def unit(i):
                        dve.wait_ge(r_ss, i + 1)
                        dve.wait_ge(r_kr, i + 1)
                        dve.tensor_tensor(kk[:, :, :], kk[:, :, :], PS[:, 6, :].rearrange("p (c n) -> p c n", c=CT),
                                          ALU.mult).then_inc(r_rn, 1)
                        dve.wait_ge(r_rn, i + 1)

                    def keys(i):
                        if i >= 1:
                            dve.wait_ge(r_pP, i)
                        link(dve.scalar_tensor_tensor(kn[:, :, :], cut(sga, i), -1.0, by_c(3), ALU.add, ALU.mult))
                        dve.scalar_tensor_tensor(kn[:, :, :], kn[:, :, :], 1.0, cut(kT, i), ALU.add, ALU.mult).then_inc(r_kp, 1)

                    def beta(i):
                        link(dve.tensor_tensor(be[:, :, :], kk[:, :, :], cut(sga, i), ALU.mult))
                        dve.wait_ge(r_exp, 3 * i + 3)
                        link(dve.tensor_tensor(be[:, :, :], be[:, :, :], eN[:, :, :], ALU.mult))

                    def alpha(i):
                        dve.wait_ge(r_kp, i + 1)
                        link(dve.tensor_tensor(ka[:, :, :], kn[:, :, :], eN[:, :, :], ALU.mult))
                        dve.tensor_tensor(ar[:, i % 2, :, 0, :], kk[:, :, :], eL[:, :, :], ALU.mult).then_inc(r_pD, 1)

                    def seq(i, s):
                        q = i % 2
                        if s in (0, 3):
                            cp = s // 3
                            rows = slice(64 * cp, 64 * cp + 64)
                            dve.wait_ge(q_R, 2 * i + cp + 1)
                            dve.tensor_copy(Rb[rows, :], PS[rows, 4, :]).then_inc(q_Re, 1)
                        if s in (2, 5):
                            cp = s // 5
                            dve.wait_ge(q_S, 2 * i + cp + 1)
                            diag = [(slice(64 * a, 64 * a + 64), S[64 * a:64 * a + 64, :, 64 * a:64 * a + 64]) for a in range(2)]
                            for a, (rows, d) in enumerate(diag):
                                g = PS[rows, 6, :].rearrange("p (c n) -> p c n", c=CT)[:, :, 64 * a:64 * a + 64]
                                link(dve.tensor_tensor(d, d, g, ALU.add))
                            for rows, d in diag:
                                m = pc[rows, q, :, cp:cp + 1].to_broadcast([64, CT, 64])
                                dve.tensor_tensor(d, d, m, ALU.mult).then_inc(q_Se, 1)
                            dve.wait_ge(q_Se, 4 * i + 2 * cp + 2)

                    def post(i, s):
                        v = ysb[:, :].rearrange("p (h n) -> p h n", n=HD)

                        def per_head(a):
                            return a.unsqueeze(2).to_broadcast([P, NG, HD])
                        if s == 0:
                            dve.wait_ge(q_y1, i + 1)
                            link(dve.tensor_reduce(gn[:, 0, :], v, AX.X, ALU.add))
                            link(dve.tensor_scalar(gn[:, 0, :], gn[:, 0, :], 1.0 / HD, None, ALU.mult))
                            link(dve.tensor_tensor(v, v, per_head(gn[:, 0, :]), ALU.subtract))
                        if s == 1:
                            link(dve.tensor_tensor(Sq[:, :, :], v, v, ALU.mult))
                            link(dve.tensor_reduce(gn[:, 1, :], Sq[:, :, :], AX.X, ALU.add))
                            link(dve.tensor_scalar(gn[:, 1, :], gn[:, 1, :], 1.0 / HD, GN_EPS, ALU.mult, ALU.add))
                            inverse_root(dve, link, gr[:, 0, :], gn[:, 1, :], gr[:, 1, :], gr[:, 2, :])
                            link(dve.tensor_tensor(v, v, per_head(gr[:, 0, :]), ALU.mult))
                        if s == 2:
                            link(dve.tensor_tensor(ysb[:, :], ysb[:, :], lng_b[:, :], ALU.mult))
                            link(dve.tensor_tensor(ysb[:, :], ysb[:, :], lnb_b[:, :], ALU.add))
                            dve.wait_ge(q_bg, i + 1)
                            link(dve.tensor_copy(gn[:, 2, :], PS[:, 6, 0:NG]))
                            link(dve.tensor_tensor(Sq[:, :, :].rearrange("p (c a) n -> p c a n", a=2),
                                                   cut(vT, i).rearrange("p c (a n) -> p c a n", a=2),
                                                   gn[:, 2, :].rearrange("p (c a) -> p c a", a=2).unsqueeze(3).to_broadcast([P, CT, 2, HD]),
                                                   ALU.mult))
                            link(dve.tensor_tensor(v, v, Sq[:, :, :], ALU.add))
                            dve.tensor_tensor(ysb[:, :], ysb[:, :], PS[:, 5, :], ALU.mult).then_inc(q_y2, 1)

                    decay(0)
                    unit(0)
                    keys(0)
                    beta(0)
                    alpha(0)
                    for i in range(NT):
                        q = i % 2
                        for n, dst in enumerate((BG, KG)):
                            for b in range(4):
                                dve.wait_ge(r_g, 8 * i + 4 * n + b + 1)
                                m = causal2[:, :, :].unsqueeze(1).to_broadcast([P, 2, 2, P])
                                dve.tensor_tensor(dst[:, q, 2 * b:2 * b + 2, :, :],
                                                  PS[:, b, :].rearrange("p (g a n) -> p g a n", g=2, a=2), m,
                                                  ALU.mult).then_inc(r_ge, 1)
                        dve.wait_ge(r_lm, NL * i + 1)
                        dve.tensor_tensor(XT[:, q, :, :], over_heads(ident[:, :], NG), LM[:, 0, :, :],
                                          ALU.subtract).then_inc(r_x0, 1)
                        if i == 0:
                            dve.reciprocal(rn[:, 2 * P:T], rn[:, 2 * P:T]).then_inc(r_ri, 1)
                        more = i + 1 < NT
                        if more:
                            decay(i + 1)
                        for l in range(1, NL):
                            if i >= 1 and l <= 3:
                                seq(i - 1, 2 * l - 2)
                            if l == 1 and more:
                                unit(i + 1)
                            if i >= 1 and l == 4:
                                post(i - 1, 0)
                            for hf in range(2):
                                dve.wait_ge(r_X, 2 * (NL - 1) * i + 2 * (l - 1) + hf + 1)
                                v = X[:, 4 * hf:4 * hf + 4, :]
                                dve.wait_ge(r_Te, 2 * NL * i + 2 + hf - 1)
                                dve.tensor_tensor(v, v, PS[:, 2 + hf, :].rearrange("p (c n) -> p c n", c=4),
                                                  ALU.subtract).then_inc(r_Xe, 1)
                            dve.wait_ge(r_Xe, 2 * (NL - 1) * i + 2 * l)
                            if i >= 1 and l <= 3:
                                seq(i - 1, 2 * l - 1)
                            if more and l == 2:
                                keys(i + 1)
                            if more and l == 3:
                                beta(i + 1)
                            if i >= 1 and l == 4:
                                post(i - 1, 1)
                        if more:
                            alpha(i + 1)
                        if i >= 1:
                            post(i - 1, 2)
                    for s in range(6):
                        seq(NT - 1, s)
                    post(NT - 1, 0)
                    post(NT - 1, 1)
                    post(NT - 1, 2)

        with ExitStack() as st:
            sbo = tile_in(st)
            attO = sbo("attO", [P, CT, T])
            wraw = [t[:, c, :] for t in (kT, vT) for c in range(CT)]
            woh, wol = sbo("woh", [P, KT, D], f32r), sbo("wol", [P, KT, D], f32r)
            mh, ml = sbo("mh", [P, 2, KT, P], f32r), sbo("ml", [P, 2, KT, P], f32r)
            g2b = sbo("g2b", [P, D])
            xo = sbo("xo", [P, 2, D])
            xn = sbo("xn", [P, 2, D])
            xn2T = sbo("xn2T", [P, KT, P])
            junk = sbo("junk", [P, D])
            rw = sbo("rw", [P, KT, NE])
            o_sq = sbo("o_sq", [P, NT])
            o_rs = sbo("o_rs", [P, 4, NT])
            lg = sbo("lg", [P, NT, NE])
            v8 = sbo("v8", [P, NT, 8])
            i8 = sbo("i8", [P, NT, 8], u32)
            ix4 = sbo("ix4", [P, NT, TOPK])
            OH = sbo("OH", [P, NT * TOPK, NE])
            pick = sbo("pick", [P, NT, NE])
            past = sbo("past", [P, NT + 1, NE])
            sv = sbo("sv", [P, NT, NE])
            e_io = sbo("e_io", [P, NE])
            e_T = sbo("e_T", [P, NE])
            pl4 = sbo("pl4", [P, TOPK, NE])
            place_u = sbo("place_u", [P, NT * TOPK], u32)
            p_io = sbo("p_io", [P, 1])
            ioi = sbo("ioi", [P, NE + 1], i32)
            cnt, nit, inc, base, tmp, first = (sbo(n, [P, NE]) for n in ("cnt", "nit", "inc", "base", "tmp", "first"))
            it = sbo("it", [P, 8])
            itab = sbo("itab", [P, 5], i32)
            gsum = sbo("gsum", [P, NT, 1])
            sf = sbo("sf", [P, NT * TOPK])
            tokid = sbo("tokid", [P, NT], u32)
            o_ws = [sem(f"o_w{n}") for n in range(2)]
            o_at, o_hi, o_lo = (sem(n) for n in ("o_at", "o_hi", "o_lo"))

            def mixed(j, half):
                return 5 * half + 1 if j == 0 else 2 * j + half + 9

            def weight(k):
                return k + 2 + k // CT

            o_w, o_mm, o_h, o_ssq, o_xn = (sem(n) for n in ("o_w", "o_mm", "o_h", "o_ssq", "o_xn"))
            o_xs = (sem("o_xs0"), sem("o_xs1"))
            o_t, o_te, o_lg, o_le, o_io = (sem(n) for n in ("o_t", "o_te", "o_lg", "o_le", "o_io"))
            o_pk, o_rk, o_dv, o_ex, o_pl, o_it, o_sc, o_itd = (sem(n) for n in ("o_pk", "o_rk", "o_dv", "o_ex", "o_pl", "o_it", "o_sc", "o_itd"))
            o_hds = (sem("o_hd0"), sem("o_hd1"))
            o_xds = (sem("o_xd0"), sem("o_xd1"))
            h_rows = h_d.rearrange("(j p) d -> j p d", p=P)
            xn_rows = xn2_d.rearrange("(j p) d -> j p d", p=P)
            with nc.Block() as block:
                @block.sync
                def _(sp):
                    w_out = A["w_out"][0].rearrange("(k p) n -> p k n", p=P)
                    sp.dma_start(kT[:, :, :], w_out[:, 0:CT, :]).then_inc(o_ws[0], 16)
                    sp.dma_start(attO[:, :, :], att_d).then_inc(o_at, 16)
                    sp.dma_start(vT[:, :, :], w_out[:, CT:KT, :]).then_inc(o_ws[1], 16)
                    for j in range(2):
                        sp.dma_start(xo[:, j, :], x_rows[j]).then_inc(o_xs[j], 16)
                    sp.dma_start(g2b[:, :], A["norm2_g"][0].partition_broadcast(P)).then_inc(o_w, 16)
                    sp.dma_start(rw[:, :, :], A["router_w"][0].rearrange("(k p) n -> p k n", p=P)).then_inc(o_w, 16)
                    for j in range(NT):
                        sp.wait_ge(o_h, j + 1)
                        sp.dma_start(h_rows[j], xo[:, j % 2, :]).then_inc(o_hds[j % 2], 16)
                        sp.wait_ge(o_xn, j + 1)
                        sp.dma_start(xn_rows[j], xn[:, j % 2, :]).then_inc(o_xds[j % 2], 16)
                        if j + 2 < NT:
                            sp.wait_ge(o_hds[j % 2], 16 * (j // 2 + 1))
                            sp.dma_start(xo[:, j % 2, :], x_rows[j + 2]).then_inc(o_xs[j % 2], 16)
                    sp.wait_ge(o_it, 1)
                    sp.dma_start(item_d, itab[:, :]).then_inc(o_itd, 16)
                    sp.wait_ge(o_itd, 16)
                    for a in range(2):
                        sp.wait_ge(o_hds[a], 16 * NT // 2)
                        sp.wait_ge(o_xds[a], 16 * NT // 2)
                    sp.wait_ge(o_sc, 16 * NT * TOPK)

                @block.tensor
                def _(pe):
                    def project(j):
                        if j >= 2:
                            pe.wait_ge(o_h, j - 1)
                        for k in range(KT):
                            if j == 0:
                                pe.wait_ge(o_lo, weight(k))
                            elif k % CT == 0:
                                pe.wait_ge(o_lo, mixed(j, k // CT))
                            for th in range(2):
                                for a, b in ((0, 0), (0, 1), (1, 0)):
                                    ins = pe.matmul(PS[:, 2 * (j % 2) + th, :], (mh, ml)[a][:, j % 2, k, :],
                                                    (woh, wol)[b][:, k, th * 512:(th + 1) * 512],
                                                    start=(k == 0 and a == b), stop=(k == KT - 1 and a == 1))
                        ins.then_inc(o_mm, 1)

                    def route(j):
                        pe.wait_ge(o_xn, j + 1)
                        if j >= 1:
                            pe.wait_ge(o_te, j)
                        for k in range(KT):
                            ins = pe.transpose(PS[:, 4 + k // 4, (k % 4) * P:(k % 4 + 1) * P],
                                               xn[:, j % 2, k * P:(k + 1) * P], ident[:, :])
                        ins.then_inc(o_t, 1)
                        pe.wait_ge(o_te, j + 1)
                        if j >= 2:
                            pe.wait_ge(o_pl, j - 1)
                        for k in range(KT):
                            ins = pe.matmul(PS[:, 6 + j % 2, 0:NE], xn2T[:, k, :], rw[:, k, :],
                                            start=(k == 0), stop=(k == KT - 1))
                        ins.then_inc(o_lg, 1)

                    def rank(j):
                        pe.wait_ge(o_pk, j + 1)
                        pe.matmul(PS[:, 6 + j % 2, 64:64 + NE], later[:, :], pick[:, j, :], start=True, stop=False)
                        ins = pe.matmul(PS[:, 6 + j % 2, 64:64 + NE], ones[:, :], past[:, j, :], start=False, stop=True)
                        if j == NT - 1:
                            ins = pe.matmul(PS[:, 2, 0:NE], ones[:, :], past[:, NT, :], start=True, stop=True)
                        ins.then_inc(o_rk, 1)

                    project(0)
                    pe.wait_ge(o_w, 32)
                    for j in range(NT):
                        if j + 1 < NT:
                            project(j + 1)
                        if j >= 2:
                            rank(j - 2)
                        route(j)
                    rank(NT - 2)
                    rank(NT - 1)

                @block.scalar
                def _(act):
                    def mix_head(j, half):
                        if j == 0 and half:
                            act.wait_ge(o_at, 16)
                        act.activation(mh[:, j % 2, CT * half:CT * half + CT, :], (rT, attO)[half][:, :, j * P:(j + 1) * P],
                                       ACT.Copy).then_inc(o_hi, 1)

                    mix_head(0, 0)
                    for k in range(KT):
                        if k == CT:
                            mix_head(0, 1)
                        if k % CT == 0:
                            act.wait_ge(o_ws[k // CT], 16)
                        act.activation(woh[:, k, :], wraw[k], ACT.Copy).then_inc(o_hi, 1)
                    for j in range(NT):
                        if j + 1 < NT:
                            if j >= 1:
                                act.wait_ge(o_mm, j)
                            mix_head(j + 1, 0)
                            mix_head(j + 1, 1)
                        act.wait_ge(o_h, j + 1)
                        act.activation(junk[:, :], xo[:, j % 2, :], ACT.Square,
                                       accum_out=o_sq[:, j:j + 1]).then_inc(o_ssq, 1)
                        act.wait_ge(o_ssq, j + 1)
                        act.wait_ge(o_t, j + 1)
                        act.activation(xn2T[:, :, :].rearrange("p k n -> p (k n)"), pair(2), ACT.Copy).then_inc(o_te, 1)
                    act.wait_ge(o_dv, 1)
                    act.activation(gates[:, :, :], gates[:, :, :], ACT.Exp).then_inc(o_ex, 1)

                @block.gpsimd
                def _(pool):
                    link = linker(pool, own_pool)
                    link(pool.iota(ioi[:, 0:NE], [[1, NE]], base=0, channel_multiplier=0))
                    link(pool.iota(ioi[:, NE:NE + 1], [[0, 1]], base=0, channel_multiplier=1))
                    link(pool.iota(tokid[:, :], [[P, NT]], base=0, channel_multiplier=1))
                    link(pool.tensor_copy(e_io[:, :], ioi[:, 0:NE]))
                    link(pool.tensor_copy(p_io[:, :], ioi[:, NE:NE + 1]))
                    pool.sem_inc(o_io, 1)
                    for n in range(NT * TOPK):
                        if n % TOPK == 0:
                            pool.wait_ge(o_pl, n // TOPK + 1)
                        pool.indirect_dma_start(token_d[:, :], bass.IndirectOffsetOnAxis(place_u[:, n:n + 1], 0),
                                                tokid[:, n // TOPK:n // TOPK + 1], None).then_inc(o_sc, 16)

                @block.vector
                def _(dve):
                    link = linker(dve, own_dve)

                    def logits(j):
                        dve.wait_ge(o_lg, j + 1)
                        dve.tensor_tensor(lg[:, j, :], PS[:, 6 + j % 2, 0:NE], rb_b[:, :], ALU.add).then_inc(o_le, 1)
                        dve.wait_ge(o_le, j + 1)
                        link(dve.max(v8[:, j, :], lg[:, j, :]))
                        link(dve.max_index(i8[:, j, :], v8[:, j, :], lg[:, j, :]))
                        link(dve.tensor_copy(ix4[:, j, :], i8[:, j, 0:TOPK]))
                        oh = OH[:, TOPK * j:TOPK * (j + 1), :]
                        link(dve.tensor_tensor(oh, e_io[:, :].unsqueeze(1).to_broadcast([P, TOPK, NE]),
                                               ix4[:, j, :].unsqueeze(2).to_broadcast([P, TOPK, NE]), ALU.is_equal))
                        link(dve.tensor_reduce(pick[:, j, :], oh.rearrange("p k e -> p e k"), AX.X, ALU.add))
                        dve.tensor_tensor(past[:, j + 1, :], past[:, j, :], pick[:, j, :], ALU.add).then_inc(o_pk, 1)
                        dve.wait_ge(o_pk, j + 1)

                    def place(j):
                        dve.wait_ge(o_rk, j + 1)
                        link(dve.tensor_tensor(sv[:, j, :], PS[:, 6 + j % 2, 64:64 + NE], e_T[:, :], ALU.add))
                        link(dve.tensor_tensor(pl4[:, :, :], OH[:, TOPK * j:TOPK * (j + 1), :],
                                               sv[:, j, :].unsqueeze(1).to_broadcast([P, TOPK, NE]), ALU.mult))
                        link(dve.tensor_reduce(sf[:, TOPK * j:TOPK * (j + 1)], pl4[:, :, :], AX.X, ALU.add))
                        dve.tensor_copy(place_u[:, TOPK * j:TOPK * (j + 1)], sf[:, TOPK * j:TOPK * (j + 1)]).then_inc(o_pl, 1)

                    def mix_rest(j, half):
                        dve.wait_ge(o_hi, mixed(j, half))
                        cut_ = (slice(None), j % 2, slice(CT * half, CT * half + CT), slice(None))
                        dve.tensor_tensor(ml[cut_], (rT, attO)[half][:, :, j * P:(j + 1) * P], mh[cut_].bitcast(f32),
                                          ALU.subtract).then_inc(o_lo, 1)

                    dve.wait_ge(o_io, 1)
                    link(dve.tensor_scalar(e_T[:, :], e_io[:, :], float(T), None, ALU.mult))
                    link(dve.memset(past[:, 0, :], 0.0))
                    mix_rest(0, 0)
                    for k in range(KT):
                        if k == CT:
                            mix_rest(0, 1)
                        dve.wait_ge(o_hi, weight(k))
                        dve.tensor_tensor(wol[:, k, :], wraw[k], woh[:, k, :].bitcast(f32), ALU.subtract).then_inc(o_lo, 1)
                    mix_rest(1, 0)
                    mix_rest(1, 1)
                    dve.wait_ge(o_w, 32)
                    for j in range(NT):
                        dve.wait_ge(o_mm, j + 1)
                        dve.wait_ge(o_xs[j % 2], 16 * (j // 2 + 1))
                        dve.tensor_tensor(xo[:, j % 2, :], xo[:, j % 2, :], pair(j % 2), ALU.add).then_inc(o_h, 1)
                        if 1 <= j < NT - 1:
                            mix_rest(j + 1, 0)
                            mix_rest(j + 1, 1)
                        dve.wait_ge(o_ssq, j + 1)
                        r = [o_rs[:, n, j:j + 1] for n in range(4)]
                        link(dve.tensor_scalar(r[1], o_sq[:, j:j + 1], 1.0 / D, NORM_EPS, ALU.mult, ALU.add))
                        inverse_root(dve, link, *r)
                        if j >= 2:
                            dve.wait_ge(o_xds[j % 2], 16 * (j // 2))
                            dve.wait_ge(o_t, j - 1)
                        dve.scalar_tensor_tensor(xn[:, j % 2, :], xo[:, j % 2, :], r[0], g2b[:, :],
                                                 ALU.mult, ALU.mult).then_inc(o_xn, 1)
                        if j >= 2:
                            place(j - 2)
                        if j >= 1:
                            logits(j - 1)
                    place(NT - 2)
                    logits(NT - 1)
                    place(NT - 1)
                    link(dve.tensor_tensor(gates[:, :, :], v8[:, :, 0:TOPK], v8[:, :, 0:1].to_broadcast([P, NT, TOPK]),
                                           ALU.subtract))
                    dve.sem_inc(o_dv, 1)
                    link(dve.tensor_copy(cnt[:, :], PS[:, 2, 0:NE]))
                    link(dve.tensor_scalar(nit[:, :], cnt[:, :], 0.0, None, ALU.is_gt))
                    for m in range(1, T // SLOTS):
                        link(dve.scalar_tensor_tensor(nit[:, :], cnt[:, :], float(SLOTS * m), nit[:, :], ALU.is_gt, ALU.add))
                    link(dve.tensor_tensor_scan(inc[:, :], ones[:, 0:NE], nit[:, :], 0.0, ALU.mult, ALU.add))
                    link(dve.tensor_tensor(base[:, :], inc[:, :], nit[:, :], ALU.subtract))
                    link(dve.tensor_scalar(base[:, :], base[:, :], float(SLOTS), None, ALU.mult))
                    link(dve.tensor_tensor_scan(first[:, :], ones[:, 0:NE], cnt[:, :], 0.0, ALU.mult, ALU.add))
                    link(dve.tensor_tensor(first[:, :], first[:, :], cnt[:, :], ALU.subtract))
                    link(dve.tensor_tensor(tmp[:, :], first[:, :], e_T[:, :], ALU.subtract))
                    link(dve.tensor_tensor(sv[:, :, :], sv[:, :, :], tmp[:, :].unsqueeze(1).to_broadcast([P, NT, NE]), ALU.add))
                    v4 = OH[:, :, :].rearrange("p (t k) e -> p t k e", k=TOPK)
                    link(dve.tensor_tensor(v4, v4, sv[:, :, :].unsqueeze(2).to_broadcast([P, NT, TOPK, NE]), ALU.mult))
                    link(dve.tensor_reduce(sf[:, :], OH[:, :, :], AX.X, ALU.add))
                    link(dve.tensor_copy(slots_u[:, :], sf[:, :]))
                    link(dve.tensor_scalar(tmp[:, :], inc[:, :], p_io[:, 0:1], None, ALU.is_le))
                    link(dve.tensor_reduce(it[:, 0:1], tmp[:, :], AX.X, ALU.add))
                    link(dve.tensor_scalar(it[:, 0:1], it[:, 0:1], float(NE - 1), None, ALU.min))
                    link(dve.tensor_scalar(tmp[:, :], e_io[:, :], it[:, 0:1], None, ALU.is_equal))
                    link(dve.tensor_tensor(cnt[:, :], cnt[:, :], base[:, :], ALU.add))
                    link(dve.tensor_tensor(first[:, :], first[:, :], base[:, :], ALU.subtract))
                    link(dve.tensor_tensor(first[:, :], tmp[:, :], first[:, :], ALU.mult))
                    link(dve.tensor_reduce(it[:, 5:6], first[:, :], AX.X, ALU.add))
                    link(dve.tensor_tensor(base[:, :], tmp[:, :], base[:, :], ALU.mult))
                    link(dve.tensor_reduce(it[:, 6:7], base[:, :], AX.X, ALU.add))
                    link(dve.tensor_tensor(tmp[:, :], tmp[:, :], cnt[:, :], ALU.mult))
                    link(dve.tensor_reduce(it[:, 3:4], tmp[:, :], AX.X, ALU.add))
                    link(dve.scalar_tensor_tensor(it[:, 4:5], p_io[:, :], -float(SLOTS), it[:, 3:4], ALU.mult, ALU.add))
                    link(dve.tensor_scalar(it[:, 1:2], it[:, 4:5], float(P), None, ALU.is_gt))
                    link(dve.tensor_copy(it[:, 2:3], inc[:, NE - 1:NE]))
                    link(dve.scalar_tensor_tensor(it[:, 3:4], p_io[:, :], float(SLOTS), it[:, 5:6], ALU.mult, ALU.add))
                    link(dve.tensor_scalar(it[:, 3:4], it[:, 3:4], float(T * TOPK), None, ALU.min))
                    link(dve.scalar_tensor_tensor(it[:, 6:7], p_io[:, :], float(SLOTS), it[:, 6:7], ALU.mult, ALU.subtract))
                    link(dve.scalar_tensor_tensor(it[:, 4:5], it[:, 0:1], float(T), it[:, 6:7], ALU.mult, ALU.add))
                    link(dve.tensor_scalar(it[:, 4:5], it[:, 4:5], float(NE * T - SLOTS), None, ALU.min))
                    link(dve.tensor_copy(itab[:, :], it[:, 0:5]))
                    dve.sem_inc(o_it, 1)
                    dve.wait_ge(o_ex, 1)
                    link(dve.tensor_reduce(gsum[:, :, :], gates[:, :, :], AX.X, ALU.add))
                    link(dve.reciprocal(gsum[:, :, :], gsum[:, :, :]))
                    link(dve.tensor_tensor(gates[:, :, :], gates[:, :, :], gsum[:, :, :].to_broadcast([P, NT, TOPK]), ALU.mult))
        mix.close()
        small.close()

        UNITS, KH = 12, KT // 2
        NRAW, NSPL = 4, 6
        BY_POOL = [2, 4]
        BY_DVE = [u for u in range(UNITS) if u not in BY_POOL]
        with ExitStack() as st:
            sbe = tile_in(st)
            raw = sbe("raw", [P, NRAW, KH, 512])
            wh = sbe("wh", [P, NSPL, KH, 512], f32r)
            wl = sbe("wl", [P, NSPL, KH, 512], f32r)
            xh = sbe("xh", [P, KT, SLOTS], f32r)
            xl = sbe("xl", [P, KT, SLOTS], f32r)
            ah = sbe("ah", [P, KT, SLOTS], f32r)
            al = sbe("al", [P, KT, SLOTS], f32r)
            xg = sbe("xg", [P, 2, D])
            hb = sbe("hb", [P, 2, 512])
            gl = sbe("gl", [P, 2, 256])
            li = sbe("li", [P, 2, 256])
            sg = sbe("sg", [P, 2, 256])
            av = sbe("av", [P, 2, 2, 256])
            yb = sbe("yb", [P, 2, D])
            bu = sbe("bu", [P, 2 * D])
            bd = sbe("bd", [P, D])
            idx = sbe("idx", [P, 2], u32)
            items_t = sbe("items_t", [1, (MAXI + 2) * 5], i32)
            e_raw = [sem(f"e_raw{n}") for n in range(NRAW)]
            e_hi, e_lo, e_used = sem("e_hi"), sem("e_lo"), sem("e_used")
            e_bank, e_gl, e_sg, e_av, e_T, e_ah, e_al = (sem(n) for n in ("e_bank", "e_gl", "e_sg", "e_av", "e_T", "e_ah", "e_al"))
            e_X, e_xh, e_xl, e_yd, e_ix, e_gt, e_lp, e_rowu, e_rowd, e_bu, e_bd = (sem(n) for n in ("e_X", "e_xh", "e_xl", "e_yd", "e_ix", "e_gt", "e_lp", "e_rowu", "e_rowd", "e_bu", "e_bd"))
            e_pw, e_tw, e_tab = sem("e_pw"), sem("e_tw"), sem("e_tab")
            w_up = A["exp_w_up"][0].rearrange("e (k p) n -> e p k n", p=P)
            w_dn = A["exp_w_down"][0].rearrange("e (k p) n -> e p k n", p=P)

            def field(eng, i, n, lo, hi):
                return eng.value_load(items_t[0:1, bass.ds(5 * i + n, 1)], min_val=lo, max_val=hi)

            def items(eng):
                return eng.value_load(items_t[0:1, 2:3], min_val=1, max_val=MAXI)

            def expert(eng, i):
                return field(eng, i, 0, 0, NE - 1)

            def first_slot(eng, i):
                return field(eng, i, 3, 0, T * TOPK)

            def by_blocks(eng, i, body):
                two = field(eng, i, 1, 0, 1)
                with eng.If(two > 0):
                    body(2)
                with eng.Else():
                    body(1)

            def wait_split(eng, i, u):
                i, u = (i - 1, u + UNITS) if u < 0 else (i, u)
                for done, us in ((e_lo, BY_DVE), (e_lp, BY_POOL)):
                    if u in us:
                        eng.wait_ge(done, len(us) * i + us.index(u) + 1)

            with nc.Block() as block:
                @block.sync
                def _(sp):
                    def load(e, i, u):
                        if not (isinstance(i, int) and u < NRAW):
                            wait_split(sp, i, u - NRAW)
                        if u < 8:
                            src = w_up[bass.ds(e, 1), :, (u % 2) * KH:(u % 2 + 1) * KH, (u // 2) * 512:(u // 2 + 1) * 512]
                        else:
                            d, kh = (u - 8) % 2, (u - 8) // 2
                            src = w_dn[bass.ds(e, 1), :, kh * KH:(kh + 1) * KH, d * 512:(d + 1) * 512]
                        sp.dma_start(raw[:, u % NRAW, :, :], src.rearrange("a p k n -> (a p) k n")).then_inc(e_raw[u % NRAW], 16)

                    sp.dma_start(items_t[0:1, :], item_d[0:MAXI + 2, :].rearrange("p n -> (p n)").unsqueeze(0)).then_inc(e_tab, 16)
                    sp.wait_ge(e_tab, 16)
                    e0 = expert(sp, 0)
                    for u in range(NSPL):
                        load(e0, 0, u)
                    with sp.Fori(0, items(sp)) as i:
                        e = expert(sp, i)
                        for u in range(NSPL, UNITS):
                            load(e, i, u)
                        en = expert(sp, i + 1)
                        for u in range(NSPL):
                            load(en, i + 1, u)

                @block.tensor
                def _(pe):
                    def unit(i, nb, u):
                        wait_split(pe, i, u)
                        if u < 8:
                            s, kh = u // 2, u % 2
                            use, left, bank = s, (xh, xl), 2 * (s % 2)
                            if u == 0:
                                pe.wait_ge(e_xl, 4 * i + 4)
                        else:
                            d, kh = (u - 8) % 2, (u - 8) // 2
                            use, left, bank = 4 + d, (ah, al), 2 * d
                            pe.wait_ge(e_al, 4 * i + 2 + 2 + 2 * kh)
                        if kh == 0:
                            pe.wait_ge(e_bank, 6 * i + use + 1)
                        for b in range(nb):
                            for n in range(KH):
                                k = kh * KH + n
                                for m, (x_, w_) in enumerate(((0, 0), (0, 1), (1, 0))):
                                    ins = pe.matmul(PS[:, bank + b, :], left[x_][:, k, b * P:(b + 1) * P],
                                                    (wh, wl)[w_][:, u % NSPL, n, :],
                                                    start=(k == 0 and m == 0), stop=(k == KT - 1 and m == 2))
                        ins.then_inc(e_used, 1)

                    def flip_x(i, x):
                        pe.wait_ge(e_gt, 32 * (i + 1))
                        pe.wait_ge(e_xl, 4 * i + x - 1)
                        for n in range(4):
                            k = (x % 2) * 4 + n
                            ins = pe.transpose(PS[:, 6 + x % 2, n * P:(n + 1) * P], xg[:, x // 2, k * P:(k + 1) * P], ident[:, :])
                        ins.then_inc(e_X, 1)

                    def flip_a(i, nb, s):
                        pe.wait_ge(e_av, 4 * i + s + 1)
                        pe.wait_ge(e_al, 4 * i + s + 1)
                        for b in range(nb):
                            for n in range(2):
                                ins = pe.transpose(PS[:, 4 + s % 2, (2 * b + n) * P:(2 * b + n + 1) * P],
                                                   av[:, s % 2, b, n * P:(n + 1) * P], ident[:, :])
                        ins.then_inc(e_T, 1)

                    for x in range(4):
                        pe.wait_ge(e_gt, 32)
                        if x >= 2:
                            pe.wait_ge(e_xl, x - 1)
                        for n in range(4):
                            k = (x % 2) * 4 + n
                            ins = pe.transpose(PS[:, 6 + x % 2, n * P:(n + 1) * P], xg[:, x // 2, k * P:(k + 1) * P], ident[:, :])
                        ins.then_inc(e_X, 1)
                    pe.wait_ge(e_tab, 16)
                    with pe.Fori(0, items(pe)) as i:
                        def body(nb):
                            for s in range(4):
                                unit(i, nb, 2 * s)
                                unit(i, nb, 2 * s + 1)
                                if s >= 1:
                                    flip_a(i, nb, s - 1)
                            unit(i, nb, 8)
                            flip_x(i + 1, 0)
                            flip_x(i + 1, 1)
                            unit(i, nb, 9)
                            flip_a(i, nb, 3)
                            flip_x(i + 1, 2)
                            flip_x(i + 1, 3)
                            unit(i, nb, 10)
                            unit(i, nb, 11)
                        by_blocks(pe, i, body)

                @block.scalar
                def _(act):
                    def head(i, u, wait=True):
                        act.wait_ge(e_raw[u % NRAW], 16 * ((UNITS // NRAW) * i + u // NRAW + 1))
                        if wait:
                            act.wait_ge(e_used, UNITS * i + u - (NSPL - 1))
                        act.activation(wh[:, u % NSPL, :, :], raw[:, u % NRAW, :, :], ACT.Copy).then_inc(e_hi, 1)

                    def x_head(i, x):
                        act.wait_ge(e_X, 4 * i + x + 1)
                        act.activation(xh[:, (x % 2) * 4:(x % 2) * 4 + 4, (x // 2) * P:(x // 2 + 1) * P],
                                       PS[:, 6 + x % 2, :].rearrange("p (k n) -> p k n", k=4), ACT.Copy).then_inc(e_xh, 1)

                    def a_head(i, nb, s):
                        act.wait_ge(e_T, 4 * i + s + 1 + 2)
                        act.activation(ah[:, 2 * s:2 * s + 2, 0:nb * P].rearrange("p k (b n) -> p b k n", b=nb),
                                       PS[:, 4 + s % 2, 0:nb * 256].rearrange("p (b k n) -> p b k n", b=nb, k=2),
                                       ACT.Copy).then_inc(e_ah, 1)

                    def sigmoid(i, nb, s):
                        act.wait_ge(e_gl, 8 * i + 2 * s + 1)
                        act.activation(sg[:, 0:nb, :], gl[:, 0:nb, :], ACT.Sigmoid, scale=1.702).then_inc(e_sg, 1)

                    for x in range(4):
                        x_head(0, x)
                    for u in range(NSPL):
                        head(0, u, wait=False)
                    act.wait_ge(e_tab, 16)
                    with act.Fori(0, items(act)) as i:
                        def body(nb):
                            for s in range(4):
                                head(i, 2 * s + NSPL) if s < 3 else head(i + 1, 0)
                                head(i, 2 * s + NSPL + 1) if s < 3 else head(i + 1, 1)
                                if s >= 1:
                                    a_head(i, nb, s - 1)
                                sigmoid(i, nb, s)
                            x_head(i + 1, 0)
                            x_head(i + 1, 1)
                            head(i + 1, 2)
                            a_head(i, nb, 3)
                            x_head(i + 1, 2)
                            x_head(i + 1, 3)
                            head(i + 1, 3)
                            head(i + 1, 4)
                            head(i + 1, 5)
                        by_blocks(act, i, body)

                @block.vector
                def _(dve):
                    def rest(i, u):
                        if u in BY_POOL:
                            return
                        dve.wait_ge(e_hi, UNITS * i + u + 1)
                        dve.tensor_tensor(wl[:, u % NSPL, :, :], raw[:, u % NRAW, :, :],
                                          wh[:, u % NSPL, :, :].bitcast(f32), ALU.subtract).then_inc(e_lo, 1)

                    def x_rest(i, x):
                        dve.wait_ge(e_xh, 4 * i + x + 1)
                        cut_ = (slice(None), slice((x % 2) * 4, (x % 2) * 4 + 4), slice((x // 2) * P, (x // 2 + 1) * P))
                        dve.tensor_tensor(xl[cut_], PS[:, 6 + x % 2, :].rearrange("p (k n) -> p k n", k=4),
                                          xh[cut_].bitcast(f32), ALU.subtract).then_inc(e_xl, 1)

                    def a_rest(i, nb, s):
                        dve.wait_ge(e_ah, 4 * i + s + 1)
                        out_, in_ = (t[:, 2 * s:2 * s + 2, 0:nb * P].rearrange("p k (b n) -> p b k n", b=nb) for t in (al, ah))
                        dve.tensor_tensor(out_, PS[:, 4 + s % 2, 0:nb * 256].rearrange("p (b k n) -> p b k n", b=nb, k=2),
                                          in_.bitcast(f32), ALU.subtract).then_inc(e_al, 1)

                    def add_up(i, nb, s):
                        dve.wait_ge(e_used, UNITS * i + 2 * s + 2)
                        dve.wait_ge(e_bu, i + 1)
                        dve.tensor_tensor(hb[:, 0:nb, :], PS[:, 2 * (s % 2):2 * (s % 2) + nb, :],
                                          bu[:, s * 512:(s + 1) * 512].unsqueeze(1).to_broadcast([P, nb, 512]),
                                          ALU.add).then_inc(e_bank, 1)

                    def glu(i, nb, s):
                        dve.wait_ge(e_gl, 8 * i + 2 * s + 2)
                        dve.wait_ge(e_T, 4 * i + s + 1)
                        dve.scalar_tensor_tensor(hb[:, 0:nb, 0:256], li[:, 0:nb, :], 1.0, gl[:, 0:nb, :],
                                                 ALU.add, ALU.mult).then_inc(e_tw, 1)
                        dve.wait_ge(e_tw, 4 * i + s + 1)
                        dve.wait_ge(e_sg, 4 * i + s + 1)
                        dve.tensor_tensor(av[:, s % 2, 0:nb, :], hb[:, 0:nb, 0:256], sg[:, 0:nb, :], ALU.mult).then_inc(e_av, 1)
                        dve.wait_ge(e_av, 4 * i + s + 1)

                    def add_dn(i, nb, d):
                        dve.wait_ge(e_used, UNITS * i + 11 + d)
                        dve.wait_ge(e_bd, i + 1)
                        if d == 0:
                            dve.wait_ge(e_yd, 16 * i + 16)
                        dve.tensor_tensor(yb[:, 0:nb, d * 512:(d + 1) * 512], PS[:, 2 * d:2 * d + nb, :],
                                          bd[:, d * 512:(d + 1) * 512].unsqueeze(1).to_broadcast([P, nb, 512]),
                                          ALU.add).then_inc(e_bank, 1)

                    dve.sem_inc(e_bank, 2)
                    dve.sem_inc(e_al, 2)
                    dve.sem_inc(e_T, 2)
                    for x in range(4):
                        x_rest(0, x)
                    for u in range(NSPL):
                        rest(0, u)
                    dve.wait_ge(e_tab, 16)
                    with dve.Fori(0, items(dve)) as i:
                        def body(nb):
                            for s in range(4):
                                rest(i, 2 * s + NSPL) if s < 3 else rest(i + 1, 0)
                                add_up(i, nb, s)
                                if s >= 1:
                                    a_rest(i, nb, s - 1)
                                rest(i, 2 * s + NSPL + 1) if s < 3 else rest(i + 1, 1)
                                glu(i, nb, s)
                            x_rest(i + 1, 0)
                            x_rest(i + 1, 1)
                            rest(i + 1, 2)
                            a_rest(i, nb, 3)
                            x_rest(i + 1, 2)
                            x_rest(i + 1, 3)
                            rest(i + 1, 3)
                            add_dn(i, nb, 0)
                            rest(i + 1, 4)
                            add_dn(i, nb, 1)
                            rest(i + 1, 5)
                        by_blocks(dve, i, body)

                @block.gpsimd
                def _(pool):
                    def hold(counter, value):
                        pool.wait_ge(counter, value)
                        pool.sem_inc(e_pw, 1)

                    def gather(i):
                        for b in range(2):
                            pool.indirect_dma_start(xg[:, b, :], None, xn2_d[:, :],
                                                    bass.IndirectOffsetOnAxis(idx[:, b:b + 1], 0)).then_inc(e_gt, 16)

                    def indices(i):
                        src = token_d[bass.ds(field(pool, i, 4, 0, NE * T - SLOTS), SLOTS), :].rearrange("(b p) a -> p (b a)", p=P)
                        with nc.allow_non_contiguous_dma(reason="token indices, 1 KiB"):
                            pool.dma_start(idx[:, :], src).then_inc(e_ix, 16)

                    def bias(e, row, dst, done):
                        pool.dma_start(dst[0:1, :], row[bass.ds(e, 1), :]).then_inc(done, 16)

                    def clamp(i, nb, s):
                        hold(e_bank, 6 * i + s + 3)
                        v = hb[:, 0:nb, :].rearrange("p b (n a) -> p b n a", a=2)
                        pool.tensor_scalar(gl[:, 0:nb, :], v[:, :, :, 0], 7.0, None, ALU.min).then_inc(e_gl, 1)
                        pool.tensor_scalar(li[:, 0:nb, :], v[:, :, :, 1], 7.0, -7.0, ALU.min, ALU.max).then_inc(e_gl, 1)

                    def rest(i, u):
                        hold(e_hi, UNITS * i + u + 1)
                        pool.tensor_tensor(wl[:, u % NSPL, :, :], raw[:, u % NRAW, :, :],
                                           wh[:, u % NSPL, :, :].bitcast(f32), ALU.subtract).then_inc(e_lp, 1)

                    pool.wait_ge(e_tab, 16)
                    e0 = expert(pool, 0)
                    indices(0)
                    pool.wait_ge(e_ix, 16)
                    gather(0)
                    pool.dma_start(pad_d, idx[:, :]).then_inc(e_yd, 16)
                    bias(e0, A["exp_b_up"][0], bu, e_rowu)
                    pool.wait_ge(e_rowu, 16)
                    pool.partition_broadcast(bu[:, :], bu[0:1, :]).then_inc(e_bu, 1)
                    pool.wait_ge(e_gt, 32)
                    indices(1)
                    for u in BY_POOL:
                        rest(0, u)
                    pool.wait_ge(e_X, 4)
                    with pool.Fori(0, items(pool)) as i:
                        e, en = expert(pool, i), expert(pool, i + 1)

                        def body(nb):
                            clamp(i, nb, 0)
                            bias(e, A["exp_b_down"][0], bd, e_rowd)
                            hold(e_X, 4 * i + 4)
                            hold(e_ix, 16 * i + 32)
                            gather(i + 1)
                            clamp(i, nb, 1)
                            hold(e_rowd, 16 * i + 16)
                            pool.partition_broadcast(bd[:, :], bd[0:1, :]).then_inc(e_bd, 1)
                            clamp(i, nb, 2)
                            clamp(i, nb, 3)
                            bias(en, A["exp_b_up"][0], bu, e_rowu)
                            hold(e_gt, 32 * i + 64)
                            indices(i + 2)
                            rest(i + 1, 2)
                            hold(e_rowu, 16 * i + 32)
                            pool.partition_broadcast(bu[:, :], bu[0:1, :]).then_inc(e_bu, 1)
                            rest(i + 1, 4)
                            hold(e_bank, 6 * i + 8)
                            rows = ys_d[bass.ds(first_slot(pool, i), nb * P), :].rearrange("(b p) d -> p b d", p=P)
                            pool.dma_start(rows, yb[:, 0:nb, :]).then_inc(e_yd, 16)
                        by_blocks(pool, i, body)
                    hold(e_yd, 16 * items(pool) + 16)
                    pool.wait_ge(e_ix, 32)

        with ExitStack() as st:
            sbc = tile_in(st)
            yg = sbc("yg", [P, 4, TOPK, D])
            hh = sbc("hh", [P, NT, D])
            fgb = sbc("fgb", [P, D])
            cj = sbc("cj", [P, D])
            c_sq = sbc("c_sq", [P, NT])
            c_rs = sbc("c_rs", [P, 4, NT])
            c_g = [sem(f"c_g{n}") for n in range(4)]
            c_h = [sem(f"c_h{n}") for n in range(4)]
            c_o = sem("c_o")
            c_f, c_a, c_s, c_n = (sem(n) for n in ("c_f", "c_a", "c_s", "c_n"))
            out_rows = out[0].rearrange("(j p) d -> j p d", p=P)
            with nc.Block() as block:
                @block.sync
                def _(sp):
                    sp.dma_start(fgb[:, :], A["final_g"].partition_broadcast(P)).then_inc(c_f, 16)
                    for j in range(NT):
                        if j == 2:
                            sp.wait_ge(c_g[0], 16 * TOPK)
                        if j == 4:
                            sp.wait_ge(c_g[1], 16 * TOPK)
                        sp.dma_start(hh[:, j, :], h_rows[j]).then_inc(c_h[j // 2], 16)
                    for j in range(NT):
                        sp.wait_ge(c_n, j + 1)
                        sp.dma_start(out_rows[j], hh[:, j, :]).then_inc(c_o, 16)
                    sp.wait_ge(c_o, 16 * NT)

                @block.gpsimd
                def _(pool):
                    for j in range(NT):
                        if j >= 4:
                            pool.wait_ge(c_a, j - 3)
                        for k in range(TOPK):
                            n = j * TOPK + k
                            pool.indirect_dma_start(yg[:, j % 4, k, :], None, ys_d[0:T * TOPK, :],
                                                    bass.IndirectOffsetOnAxis(slots_u[:, n:n + 1], 0)).then_inc(c_g[j % 4], 16)

                @block.vector
                def _(dve):
                    link = linker(dve, own_dve)

                    def add_rows(j):
                        h = hh[:, j, :]
                        dve.wait_ge(c_h[j // 2], 32)
                        dve.wait_ge(c_g[j % 4], 16 * TOPK * (j // 4 + 1))
                        for k in range(TOPK):
                            ins = dve.scalar_tensor_tensor(h, yg[:, j % 4, k, :], gates[:, j, k:k + 1], h, ALU.mult, ALU.add)
                            if k + 1 < TOPK:
                                link(ins)
                        ins.then_inc(c_a, 1)

                    def norm(j):
                        dve.wait_ge(c_s, j + 2)
                        r = [c_rs[:, n, j:j + 2] for n in range(4)]
                        link(dve.tensor_scalar(r[1], c_sq[:, j:j + 2], 1.0 / D, NORM_EPS, ALU.mult, ALU.add))
                        inverse_root(dve, link, *r)
                        for m in (j, j + 1):
                            dve.scalar_tensor_tensor(hh[:, m, :], hh[:, m, :], c_rs[:, 0, m:m + 1], fgb[:, :],
                                                     ALU.mult, ALU.mult).then_inc(c_n, 1)

                    dve.wait_ge(c_f, 16)
                    for j in range(0, NT, 2):
                        add_rows(j)
                        if j >= 2:
                            norm(j - 2)
                        add_rows(j + 1)
                    norm(NT - 2)

                @block.scalar
                def _(act):
                    for j in range(NT):
                        act.wait_ge(c_a, j + 1)
                        act.activation(cj[:, :], hh[:, j, :], ACT.Square, accum_out=c_sq[:, j:j + 1]).then_inc(c_s, 1)
                        act.wait_ge(c_s, j + 1)


_OUTS = [((1, 1024, 1024), 'float32')]


def kernel(**inputs):
    import numpy as _np
    import concourse.bacc as _bacc
    from concourse import mybir as _mybir
    from concourse.bass_utils import run_bass_kernel_spmd as _run

    nc = _bacc.Bacc("TRN2", target_bir_lowering=False, num_devices=1)
    arrays, args = {}, {}
    for name in inputs:
        a = _np.ascontiguousarray(inputs[name])
        arrays[f"in_{name}_dram"] = a
        args[name] = nc.dram_tensor(f"in_{name}_dram", a.shape, _mybir.dt.from_np(a.dtype), kind="ExternalInput").ap()
    shape, dtype = _OUTS[0]
    out = nc.dram_tensor("out_0_dram", shape, _mybir.dt.from_np(_np.dtype(dtype)), kind="ExternalOutput").ap()
    layer_program(nc, args, out)
    r = _run(nc, [arrays], core_ids=[0])
    return r.results[0]["out_0_dram"]
```
